# Optimizing a Trainium2 kernel written in Bass

```python
import math
import jax, jax.numpy as jnp
from jax import lax
import numpy as np

D_MODEL = 1024
BATCH = 1
SEQ = 512
DEPTH = 1

GRID_W = 64
PLE_DIM = 256
ATT_HEADS = 8
ATT_KV_HEADS = 2
HEAD_DIM = 128
Q_BLOCK = 128
ROPE_THETA = 10000.0
DN_HEADS = 8
DN_DK = 128
DN_DV = 128
CONV_K = 5
CHUNK = 64
EPS = 1e-6

ATT_W = ATT_HEADS * HEAD_DIM
KV_W = ATT_KV_HEADS * HEAD_DIM
DN_KW = DN_HEADS * DN_DK
DN_VW = DN_HEADS * DN_DV
IN_SIZES = (ATT_W, KV_W, KV_W, ATT_W,
            DN_KW, DN_KW, DN_VW, 2 * DN_HEADS, 2 * DN_HEADS, DN_VW,
            D_MODEL, D_MODEL)
IN_W = ATT_W + 2 * KV_W + ATT_W + 2 * DN_KW + DN_VW + 4 * DN_HEADS + DN_VW + 2 * D_MODEL


def rms_norm(x, w):
    xf = x.astype(jnp.float32)
    y = xf * lax.rsqrt(jnp.mean(xf * xf, axis=-1, keepdims=True) + EPS)
    return (y * w.astype(jnp.float32)).astype(x.dtype)

def l2_norm(x):
    xf = x.astype(jnp.float32)
    return xf * lax.rsqrt(jnp.sum(xf * xf, axis=-1, keepdims=True) + EPS)

def split_cols(t):
    outs, start = [], 0
    for size in IN_SIZES:
        outs.append(t[..., start:start + size])
        start += size
    return outs

def axial_rope_angles(seq_len):
    rows = seq_len // GRID_W
    row = jnp.broadcast_to(jnp.arange(rows)[:, None], (rows, GRID_W)).reshape(seq_len)
    col = jnp.broadcast_to(jnp.arange(GRID_W)[None, :], (rows, GRID_W)).reshape(seq_len)
    n_freq = HEAD_DIM // 4
    inv_freq = ROPE_THETA ** (-jnp.arange(n_freq, dtype=jnp.float32) / n_freq)
    ang = jnp.concatenate([row.astype(jnp.float32)[:, None] * inv_freq,
                           col.astype(jnp.float32)[:, None] * inv_freq], axis=-1)
    return jnp.cos(ang), jnp.sin(ang)

def apply_rope(x, cos, sin):
    xf = x.astype(jnp.float32).reshape(*x.shape[:-1], HEAD_DIM // 2, 2)
    x0, x1 = xf[..., 0], xf[..., 1]
    out = jnp.stack([x0 * cos - x1 * sin, x0 * sin + x1 * cos], axis=-1)
    return out.reshape(x.shape).astype(x.dtype)

def gqa_attention(q, k, v):
    B, Hq, S, D = q.shape
    G = Hq // ATT_KV_HEADS
    nb = S // Q_BLOCK
    qb = q.reshape(B, ATT_KV_HEADS, G, nb, Q_BLOCK, D).transpose(3, 0, 1, 2, 4, 5)
    scale = D ** -0.5

    def block(qi):
        s = jnp.einsum('bkgqd,bksd->bkgqs', qi, k).astype(jnp.float32) * scale
        pr = jax.nn.softmax(s, axis=-1).astype(v.dtype)
        return jnp.einsum('bkgqs,bksd->bkgqd', pr, v)

    o = lax.map(block, qb)
    return o.transpose(1, 2, 3, 0, 4, 5).reshape(B, Hq, S, D)

def short_conv(x, w):
    C = x.shape[-1]
    return lax.conv_general_dilated(
        x, w[:, None, :].astype(x.dtype), window_strides=(1,),
        padding=((CONV_K // 2, CONV_K // 2),),
        dimension_numbers=('NWC', 'WIO', 'NWC'), feature_group_count=C)

def chunk_gated_delta_rule(q, k, v, g, beta):
    B, H, S, DK = q.shape
    DV = v.shape[-1]
    n = S // CHUNK
    q = q.reshape(B, H, n, CHUNK, DK)
    k = k.reshape(B, H, n, CHUNK, DK)
    v = v.reshape(B, H, n, CHUNK, DV)
    beta = beta.reshape(B, H, n, CHUNK)
    g = jnp.cumsum(g.reshape(B, H, n, CHUNK), axis=-1)
    tril = jnp.tril(jnp.ones((CHUNK, CHUNK), dtype=bool))
    eye = jnp.eye(CHUNK, dtype=jnp.float32)
    decay = jnp.exp(jnp.where(tril, g[..., :, None] - g[..., None, :], -jnp.inf))
    k_beta = k * beta[..., None]
    v_beta = v * beta[..., None]
    L = jnp.tril(jnp.einsum('bhncd,bhnjd->bhncj', k_beta, k) * decay, -1)
    T = lax.linalg.triangular_solve(eye + L, jnp.broadcast_to(eye, L.shape),
                                    left_side=True, lower=True, unit_diagonal=True)
    u = jnp.einsum('bhncj,bhnjv->bhncv', T, v_beta)
    w = jnp.einsum('bhncj,bhnjd->bhncd', T, k_beta * jnp.exp(g)[..., None])
    a_intra = jnp.einsum('bhncd,bhnjd->bhncj', q, k) * decay

    def step(state, xs):
        q_c, k_c, u_c, w_c, g_c, a_c = xs
        g_last = g_c[..., -1]
        v_new = u_c - jnp.einsum('bhcd,bhdv->bhcv', w_c, state)
        o = (jnp.einsum('bhcd,bhdv->bhcv', q_c * jnp.exp(g_c)[..., None], state)
             + jnp.einsum('bhcj,bhjv->bhcv', a_c, v_new))
        k_dec = k_c * jnp.exp(g_last[..., None] - g_c)[..., None]
        state = state * jnp.exp(g_last)[..., None, None] + jnp.einsum('bhcd,bhcv->bhdv', k_dec, v_new)
        return state, o

    front = lambda t: jnp.moveaxis(t, 2, 0)
    xs = (front(q), front(k), front(u), front(w), front(g), front(a_intra))
    state0 = jnp.zeros((B, H, DK, DV), jnp.float32)
    _, o = lax.scan(step, state0, xs)
    return jnp.moveaxis(o, 0, 2).reshape(B, H, S, DV)

def bidir_gated_deltanet(q, k, v, g, beta):
    flip = lambda t: jnp.flip(t, axis=2)
    o_f = chunk_gated_delta_rule(q, k, v, g[0], beta[0])
    o_b = flip(chunk_gated_delta_rule(flip(q), flip(k), flip(v), flip(g[1]), flip(beta[1])))
    return o_f + o_b

def first_inputs(seed: int = 0) -> dict:
    key = jax.random.key(seed)
    ks = jax.random.split(key, 20)
    nrm = lambda k, shape, scale: jax.random.normal(k, shape, jnp.float32) * scale
    gain = lambda k, shape: 1.0 + 0.02 * jax.random.normal(k, shape, jnp.float32)
    dt = jnp.exp(jax.random.uniform(ks[8], (DEPTH, 2, DN_HEADS), jnp.float32,
                                    math.log(1e-3), math.log(1e-1)))
    return {
        'x': nrm(ks[0], (BATCH, SEQ, D_MODEL), 1.0),
        'p': nrm(ks[1], (DEPTH, BATCH, SEQ, PLE_DIM), 1.0),
        'norm_pre': gain(ks[2], (DEPTH, D_MODEL)),
        'w_in': nrm(ks[3], (DEPTH, D_MODEL, IN_W), D_MODEL ** -0.5),
        'q_norm': gain(ks[4], (DEPTH, HEAD_DIM)),
        'k_norm': gain(ks[5], (DEPTH, HEAD_DIM)),
        'conv_w': nrm(ks[6], (DEPTH, CONV_K, 2 * DN_KW + DN_VW), CONV_K ** -0.5),
        'a_log': jnp.log(jax.random.uniform(ks[7], (DEPTH, 2, DN_HEADS), jnp.float32, 1.0, 16.0)),
        'dt_bias': dt + jnp.log(-jnp.expm1(-dt)),
        'dn_norm': gain(ks[9], (DEPTH, DN_DV)),
        'w_br_att': nrm(ks[10], (DEPTH, ATT_W, D_MODEL), ATT_W ** -0.5),
        'w_br_dn': nrm(ks[11], (DEPTH, DN_VW, D_MODEL), DN_VW ** -0.5),
        'w_out': nrm(ks[12], (DEPTH, D_MODEL, D_MODEL), D_MODEL ** -0.5),
        'norm_post': gain(ks[13], (DEPTH, D_MODEL)),
        'w_ple_proj': nrm(ks[14], (DEPTH, PLE_DIM, D_MODEL), PLE_DIM ** -0.5),
        'w_ple_gate': nrm(ks[15], (DEPTH, D_MODEL, D_MODEL), D_MODEL ** -0.5),
        'ple_norm': gain(ks[16], (DEPTH, D_MODEL)),
    }

def first_block(x, p, norm_pre, w_in, q_norm, k_norm, conv_w, a_log, dt_bias, dn_norm,
              w_br_att, w_br_dn, w_out, norm_post, w_ple_proj, w_ple_gate, ple_norm):
    B, S, _ = x.shape
    cos, sin = axial_rope_angles(S)
    heads = lambda t, nh, hd: t.reshape(B, S, nh, hd).transpose(0, 2, 1, 3)
    for i in range(DEPTH):
        h = rms_norm(x, norm_pre[i])
        (aq, ak, av, az, dq, dk, dv, db, da, dz, gate_att, gate_dn) = split_cols(h @ w_in[i])

        q = apply_rope(rms_norm(heads(aq, ATT_HEADS, HEAD_DIM), q_norm[i]), cos, sin)
        k = apply_rope(rms_norm(heads(ak, ATT_KV_HEADS, HEAD_DIM), k_norm[i]), cos, sin)
        v = heads(av, ATT_KV_HEADS, HEAD_DIM)
        o_att = gqa_attention(q, k, v).transpose(0, 2, 1, 3).reshape(B, S, ATT_W)
        y_att = (o_att * jax.nn.silu(az)) @ w_br_att[i]

        qkv = jax.nn.silu(short_conv(jnp.concatenate([dq, dk, dv], axis=-1), conv_w[i]))
        cq, ck, cv = qkv[..., :DN_KW], qkv[..., DN_KW:2 * DN_KW], qkv[..., 2 * DN_KW:]
        qd = l2_norm(heads(cq, DN_HEADS, DN_DK)) * (DN_DK ** -0.5)
        kd = l2_norm(heads(ck, DN_HEADS, DN_DK))
        vd = heads(cv, DN_HEADS, DN_DV).astype(jnp.float32)
        da4 = da.astype(jnp.float32).reshape(B, S, 2, DN_HEADS)
        db4 = db.astype(jnp.float32).reshape(B, S, 2, DN_HEADS)
        g = -jnp.exp(a_log[i].astype(jnp.float32)) * jax.nn.softplus(da4 + dt_bias[i].astype(jnp.float32))
        beta = jax.nn.sigmoid(db4)
        g = g.transpose(2, 0, 3, 1)
        beta = beta.transpose(2, 0, 3, 1)
        o_dn = bidir_gated_deltanet(qd, kd, vd, g, beta).astype(x.dtype)
        o_dn = rms_norm(o_dn.transpose(0, 2, 1, 3), dn_norm[i]).reshape(B, S, DN_VW)
        y_dn = (o_dn * jax.nn.silu(dz)) @ w_br_dn[i]

        mix = (jax.nn.sigmoid(gate_att) * y_att + jax.nn.sigmoid(gate_dn) * y_dn) @ w_out[i]
        x = x + rms_norm(mix, norm_post[i])

        e = p[i] @ w_ple_proj[i]
        x = x + rms_norm(jax.nn.sigmoid(x @ w_ple_gate[i]) * e, ple_norm[i])
    return x


DEPTH_2 = 2

N_MIXERS = 2
SB_HEADS = 16
SB_HEAD_DIM = D_MODEL // SB_HEADS
DIFF_HEADS = 8
DIFF_HEAD_DIM = D_MODEL // (2 * DIFF_HEADS)
DIFF_V_DIM = 2 * DIFF_HEAD_DIM
ROPE_THETA_2 = 500000.0
ROT_DIM = DIFF_HEAD_DIM // 4
D_FF = -(-8 * D_MODEL // (3 * 256)) * 256
NEG_INF = -1e30
N_SB = (DEPTH_2 + 1) // 2
N_DIFF = DEPTH_2 // 2


def rms_norm_2(x, g):
    xf = x.astype(jnp.float32)
    y = xf * lax.rsqrt(jnp.mean(xf * xf, axis=-1, keepdims=True) + EPS)
    return (y * g.astype(jnp.float32)).astype(x.dtype)

def partial_rope(x, positions):
    half = ROT_DIM // 2
    inv_freq = ROPE_THETA_2 ** (-jnp.arange(0, ROT_DIM, 2, dtype=jnp.float32) / ROT_DIM)
    ang = positions.astype(jnp.float32)[..., None] * inv_freq
    cos = jnp.cos(ang)[:, :, None, :]
    sin = jnp.sin(ang)[:, :, None, :]
    xr = x[..., :ROT_DIM].astype(jnp.float32)
    x1, x2 = xr[..., :half], xr[..., half:]
    rot = jnp.concatenate([x1 * cos - x2 * sin, x2 * cos + x1 * sin], axis=-1)
    return jnp.concatenate([rot.astype(x.dtype), x[..., ROT_DIM:]], axis=-1)

def _query_blocks(t):
    b, s, h, d = t.shape
    return jnp.moveaxis(t.reshape(b, s // Q_BLOCK, Q_BLOCK, h, d), 1, 0)

def _merge_blocks(o):
    nb, b, qb, h, d = o.shape
    return jnp.moveaxis(o, 0, 1).reshape(b, nb * qb, h * d)

def stick_breaking_attention(q, k, v):
    seq = k.shape[1]
    scale = SB_HEAD_DIM ** -0.5
    key_pos = jnp.arange(seq, dtype=jnp.int32)

    def block(args):
        q_blk, blk = args
        q_pos = blk * Q_BLOCK + jnp.arange(Q_BLOCK, dtype=jnp.int32)
        z = jnp.einsum('bqhd,bkhd->bhqk', q_blk, k, preferred_element_type=jnp.float32) * scale
        earlier = key_pos[None, :] < q_pos[:, None]
        log_keep = jnp.where(earlier, jax.nn.log_sigmoid(-z), 0.0)
        log_after = lax.cumsum(log_keep, axis=3, reverse=True) - log_keep
        weight = jnp.where(earlier, jnp.exp(jax.nn.log_sigmoid(z) + log_after), 0.0)
        return jnp.einsum('bhqk,bkhd->bqhd', weight.astype(v.dtype), v)

    out = lax.map(block, (_query_blocks(q), jnp.arange(seq // Q_BLOCK, dtype=jnp.int32)))
    return _merge_blocks(out)

def differential_attention(q1, q2, k1, k2, v, lam):
    seq = k1.shape[1]
    scale = DIFF_HEAD_DIM ** -0.5
    key_chunk = jnp.arange(seq, dtype=jnp.int32) // CHUNK

    def block(args):
        q1_blk, q2_blk, blk = args
        q_chunk = (blk * Q_BLOCK + jnp.arange(Q_BLOCK, dtype=jnp.int32)) // CHUNK
        visible = key_chunk[None, :] <= q_chunk[:, None]

        def attn_map(qb, kk):
            s = jnp.einsum('bqhd,bkhd->bhqk', qb, kk, preferred_element_type=jnp.float32) * scale
            return jax.nn.softmax(jnp.where(visible, s, NEG_INF), axis=-1)

        a = attn_map(q1_blk, k1) - lam * attn_map(q2_blk, k2)
        return jnp.einsum('bhqk,bkhd->bqhd', a.astype(v.dtype), v)

    out = lax.map(block, (_query_blocks(q1), _query_blocks(q2),
                          jnp.arange(seq // Q_BLOCK, dtype=jnp.int32)))
    return _merge_blocks(out)

def stick_breaking_mixer(h, w_in, w_out):
    b, s, _ = h.shape
    q, k, v = jnp.split(jnp.einsum('bsd,de->bse', h, w_in), 3, axis=-1)
    shape = (b, s, SB_HEADS, SB_HEAD_DIM)
    o = stick_breaking_attention(q.reshape(shape), k.reshape(shape), v.reshape(shape))
    return jnp.einsum('bse,ed->bsd', o, w_out)

def diff_mixer(h, positions, w_in, w_out, q_g, k_g, lq1, lk1, lq2, lk2, sub_g, layer_idx):
    b, s, _ = h.shape
    q, k, v = jnp.split(jnp.einsum('bsd,de->bse', h, w_in), 3, axis=-1)
    q = rms_norm_2(q.reshape(b, s, DIFF_HEADS, 2, DIFF_HEAD_DIM), q_g)
    k = rms_norm_2(k.reshape(b, s, DIFF_HEADS, 2, DIFF_HEAD_DIM), k_g)
    q1 = partial_rope(q[..., 0, :], positions)
    q2 = partial_rope(q[..., 1, :], positions)
    k1 = partial_rope(k[..., 0, :], positions)
    k2 = partial_rope(k[..., 1, :], positions)
    v = v.reshape(b, s, DIFF_HEADS, DIFF_V_DIM)
    lam_init = 0.8 - 0.6 * math.exp(-0.3 * layer_idx)
    lam = (jnp.exp(jnp.sum(lq1.astype(jnp.float32) * lk1.astype(jnp.float32)))
           - jnp.exp(jnp.sum(lq2.astype(jnp.float32) * lk2.astype(jnp.float32))) + lam_init)
    o = differential_attention(q1, q2, k1, k2, v, lam)
    o = rms_norm_2(o.reshape(b, s, DIFF_HEADS, DIFF_V_DIM), sub_g) * (1.0 - lam_init)
    return jnp.einsum('bse,ed->bsd', o.reshape(b, s, DIFF_HEADS * DIFF_V_DIM), w_out)

def swiglu_ffn(h, w_gate, w_up, w_down):
    g = jnp.einsum('bsd,df->bsf', h, w_gate)
    u = jnp.einsum('bsd,df->bsf', h, w_up)
    return jnp.einsum('bsf,fd->bsd', jax.nn.silu(g) * u, w_down)

def second_inputs(seed: int = 0) -> dict:
    key = jax.random.key(seed)
    ks = jax.random.split(key, 16)
    f32 = jnp.float32
    d_attn = 3 * D_MODEL

    def normal(k, shape, scale):
        return jax.random.normal(k, shape, dtype=f32) * scale

    def gain(k, shape):
        return 1.0 + 0.02 * jax.random.normal(k, shape, dtype=f32)

    x = jax.random.normal(ks[0], (BATCH, SEQ, D_MODEL), dtype=f32)
    start = jax.random.randint(ks[1], (BATCH, 1), 0, 4096, dtype=jnp.int32)
    positions = start + jnp.arange(SEQ, dtype=jnp.int32)[None, :]
    return {
        'x': x,
        'positions': positions,
        'attn_norm': gain(ks[2], (DEPTH_2, D_MODEL)),
        'w_in': normal(ks[3], (DEPTH_2, D_MODEL, d_attn), D_MODEL ** -0.5),
        'w_out': normal(ks[4], (DEPTH_2, D_MODEL, D_MODEL), D_MODEL ** -0.5),
        'q_norm': gain(ks[5], (N_DIFF, DIFF_HEAD_DIM)),
        'k_norm': gain(ks[6], (N_DIFF, DIFF_HEAD_DIM)),
        'lambda_q1': normal(ks[7], (N_DIFF, DIFF_HEAD_DIM), 0.1),
        'lambda_k1': normal(ks[8], (N_DIFF, DIFF_HEAD_DIM), 0.1),
        'lambda_q2': normal(ks[9], (N_DIFF, DIFF_HEAD_DIM), 0.1),
        'lambda_k2': normal(ks[10], (N_DIFF, DIFF_HEAD_DIM), 0.1),
        'sub_norm': gain(ks[11], (N_DIFF, DIFF_V_DIM)),
        'ffn_norm': gain(ks[12], (DEPTH_2, D_MODEL)),
        'w_gate': normal(ks[13], (DEPTH_2, D_MODEL, D_FF), D_MODEL ** -0.5),
        'w_up': normal(ks[14], (DEPTH_2, D_MODEL, D_FF), D_MODEL ** -0.5),
        'w_down': normal(ks[15], (DEPTH_2, D_FF, D_MODEL), D_FF ** -0.5),
    }

def second_block(x, positions, attn_norm, w_in, w_out, q_norm, k_norm, lambda_q1, lambda_k1,
              lambda_q2, lambda_k2, sub_norm, ffn_norm, w_gate, w_up, w_down):
    for i in range(DEPTH_2):
        h = rms_norm_2(x, attn_norm[i])
        if i % N_MIXERS == 0:
            mix = stick_breaking_mixer(h, w_in[i], w_out[i])
        else:
            j = i // N_MIXERS
            mix = diff_mixer(h, positions, w_in[i], w_out[i], q_norm[j], k_norm[j],
                             lambda_q1[j], lambda_k1[j], lambda_q2[j], lambda_k2[j],
                             sub_norm[j], i)
        x = x + mix
        x = x + swiglu_ffn(rms_norm_2(x, ffn_norm[i]), w_gate[i], w_up[i], w_down[i])
    return x


def setup_inputs(seed=0):
    out = dict(first_inputs(seed))
    for name, value in second_inputs(seed + 1).items():
        if name != "x":
            out[name + "_2"] = value
    return out


def reference(
    x, p, norm_pre, w_in, q_norm, k_norm, conv_w, a_log, dt_bias, dn_norm, w_br_att, w_br_dn,
    w_out, norm_post, w_ple_proj, w_ple_gate, ple_norm, positions_2, attn_norm_2, w_in_2,
    w_out_2, q_norm_2, k_norm_2, lambda_q1_2, lambda_k1_2, lambda_q2_2, lambda_k2_2, sub_norm_2,
    ffn_norm_2, w_gate_2, w_up_2, w_down_2,
):
    x = first_block(
        x, p, norm_pre, w_in, q_norm, k_norm, conv_w, a_log, dt_bias, dn_norm, w_br_att,
        w_br_dn, w_out, norm_post, w_ple_proj, w_ple_gate, ple_norm,
    )
    return second_block(
        x, positions_2, attn_norm_2, w_in_2, w_out_2, q_norm_2, k_norm_2, lambda_q1_2,
        lambda_k1_2, lambda_q2_2, lambda_k2_2, sub_norm_2, ffn_norm_2, w_gate_2, w_up_2,
        w_down_2,
    )


_drawn_inputs = setup_inputs


def setup_inputs(seed=0):
    import zlib

    import numpy as np

    out = dict(_drawn_inputs(seed))
    spreads = {}
    factors = {'q_norm': 8.0,
     'k_norm': 8.0,
     'dn_norm': 3.491,
     'norm_post': 3.733,
     'ple_norm': 4.334,
     'attn_norm_2': 4.256,
     'q_norm_2': 8.0,
     'k_norm_2': 8.0,
     'lambda_q1_2': 4.366,
     'lambda_k1_2': 3.401,
     'lambda_q2_2': 3.251,
     'lambda_k2_2': 8.0,
     'sub_norm_2': 146.119,
     'ffn_norm_2': 4.393}
    for name, (base, spread) in spreads.items():
        noise = np.random.default_rng([zlib.crc32(name.encode()), seed]).standard_normal(out[name].shape)
        drawn = base * np.exp(spread * noise) if base else spread * noise
        out[name] = __import__('jax').numpy.asarray(drawn.astype(out[name].dtype))
    for name, factor in factors.items():
        out[name] = (out[name] * factor).astype(out[name].dtype)
    return out
```

```python
import math
from contextlib import ExitStack

import numpy as np
import concourse.bass as bass
from concourse import mybir

F32 = mybir.dt.float32
F32R = mybir.dt.float32r
I32 = mybir.dt.int32
ALU = mybir.AluOpType
ACT = mybir.ActivationFunctionType
AX_X = mybir.AxisListType.X

S = 512
KT = 8
EPS = 1e-6
FFN_HALF = 11
LAM_INIT = 0.8 - 0.6 * math.exp(-0.3)
MAGIC = 12582912.0
TWO_PI = 2.0 * math.pi
PI_A = 6.28125
PI_B = 2029.0 / 2 ** 20
PI_C = TWO_PI - PI_A - PI_B
SET_LN_EXP = 6

CONST_NAMES = ["ones", "ident", "blk64", "rot_a", "rot_b", "tri_u", "tri_l", "neg_tri_l", "neg_ones",
               "strict_u", "neg_ge", "neg64", "lev01", "lev23", "lev4i"]

VECS = {}
_at = 0
for _n, _w in (("norm_pre", 8), ("norm_post", 8), ("ple_norm", 8), ("attn0", 8), ("attn1", 8), ("ffn0", 8),
               ("ffn1", 8), ("q_norm", 1), ("k_norm", 1), ("dn_norm", 1), ("sub_norm", 1), ("q2", 1), ("k2", 1),
               ("conv", 120), ("a_log", 16), ("dt_bias", 16), ("lq1", 64), ("lk1", 64), ("lq2", 64), ("lk2", 64),
               ("invf", 1)):
    VECS[_n] = (_at, _w)
    _at += _w
NVEC = _at
RELOAD_AT = 5
MARGIN = 0.4


PRIORITY = {"scan": 0, "out": 1, "lev0": 1, "lev1": 1, "prep": 2}


class Queue:

    def __init__(self, sem):
        self.sem, self.n, self.items, self.waited = sem, 0, [], {}
        self.clock, self.latest = 0.0, 0.0

    def wait(self, *toks):
        for t in toks:
            if t is None:
                continue
            if isinstance(t, (list, tuple)) and not isinstance(t, Tok):
                self.wait(*t)
                continue
            self.clock = max(self.clock, t.time + 0.06)
            if self.waited.get(id(t.sem), 0) < t.value:
                self.waited[id(t.sem)] = t.value
                self.items.append(("wait", t.sem, t.value))

    def do(self, fn, *after, cost=0.1):
        self.wait(*after)
        self.n += 1
        self.clock += cost
        self.latest = self.clock
        self.items.append(("inc", fn, self.sem, 1))
        return Tok(self.sem, self.n, self.clock)

    def raw(self, fn, *after, cost=0.1):
        self.wait(*after)
        self.clock += cost
        self.latest = self.clock
        self.items.append(("raw", fn))

    def mark_last(self):
        kind, fn = self.items[-1]
        assert kind == "raw"
        self.n += 1
        self.items[-1] = ("inc", fn, self.sem, 1)
        return Tok(self.sem, self.n, self.clock)

    def dma(self, fn, line, *after):
        self.wait(*after)
        line.n += 16
        self.clock += 3.0
        self.items.append(("inc", fn, line.sem, 16))
        return Tok(line.sem, line.n, self.clock + 2.0)

    def emit(self, eng):
        for it in self.items:
            if it[0] == "wait":
                eng.wait_ge(it[1], it[2])
            elif it[0] == "inc":
                it[1](eng).then_inc(it[2], it[3])
            else:
                it[1](eng)


class Tok:

    def __init__(self, sem, value, time=0.0):
        self.sem, self.value, self.time = sem, value, time


class Line:
    def __init__(self, sem):
        self.sem, self.n = sem, 0


class Slot:
    def __init__(self, ap):
        self.ap, self.free = ap, ()


class Ring:

    def __init__(self, aps):
        self.slots, self.i = [Slot(a) for a in aps], -1

    def ready(self):
        return any(s.free is not None for s in self.slots)

    def next(self):
        for _ in self.slots:
            self.i += 1
            s = self.slots[self.i % len(self.slots)]
            if s.free is not None:
                break
        assert s.free is not None, "taken before it was given back"
        free, s.free = s.free, None
        return s, free


def build(nc, wstream, wba, consts, vecs, cossin, pos, xT, pT, outT):
    ctx = ExitStack()
    with ctx:
        def sb(name, shape, dt=F32):
            return ctx.enter_context(nc.sbuf_tensor(name, shape, dt))

        def sem(name):
            return ctx.enter_context(nc.semaphore(name))

        PE, DV, AC, PO, SP = (Queue(sem(n)) for n in ("pe", "dve", "act", "pool", "sp"))

        NRAW, NSPL = 2, 2
        raw = sb("raw", [128, NRAW, 2048])
        spl = sb("spl", [128, NSPL, 2, 2048], F32R)
        x = sb("x", [128, KT, S])
        hh = sb("hh", [128, KT, S], F32R)
        hl = sb("hl", [128, KT, S], F32R)
        cst = sb("cst", [128, len(CONST_NAMES), 128])
        vec = sb("vec", [128, NVEC])
        pad = sb("pad", [128, 2, 520])
        small = sb("small", [128, 640])
        gTh = sb("gTh", [16, S], F32R)
        gTl = sb("gTl", [16, S], F32R)
        ident_r = sb("ident_r", [128, 128], F32R)
        NA = 41
        with nc.sbuf_tensor("arena", [128, NA, S], F32) as arena:
            pass
        arena_r = sb("arena_r", [128, NA, S], F32R)
        psum = [ctx.enter_context(nc.psum_tensor(f"ps{i}", [128, S], F32)) for i in range(8)]

        def A(i, n=None):
            return arena[:, i, :] if n is None else arena[:, i:i + n, :]

        def R(i):
            return arena_r[:, i, :]

        C = {n: cst[:, i, :] for i, n in enumerate(CONST_NAMES)}

        def V(name, j=0, n=1):
            a = VECS[name][0] + j
            return vec[:, a:a + n]

        eps = small[:, 0:1]
        lam_n = small[:, 1:2]
        sm_at = [2]

        def cols(n):
            a = sm_at[0]
            sm_at[0] += n
            assert sm_at[0] <= 640
            return small[:, a:a + n]

        def width(ap):
            return math.prod(ap.shape[1:])

        def cost_of(q, out, per=1.04):
            if q is AC:
                return 0.16 + 0.0007 * width(out)
            if q is PO:
                return 0.15 + 0.002 * width(out)
            return 0.07 + 0.001 * per * width(out)

        def tt(q, out, a, b, op, *after):
            return q.do(lambda e: e.tensor_tensor(out, a, b, op), *after, cost=cost_of(q, out))

        def ts(q, out, a, s1, s2, op0, op1, *after):
            if s2 is None:
                return q.do(lambda e: e.tensor_scalar(out, a, s1, None, op0), *after, cost=cost_of(q, out, 0.7))
            return q.do(lambda e: e.tensor_scalar(out, a, s1, s2, op0, op1), *after, cost=cost_of(q, out, 0.7))

        def stt(out, a, s1, b, op0, op1, *after):
            return DV.do(lambda e: e.scalar_tensor_tensor(out=out, in0=a, scalar=s1, in1=b, op0=op0, op1=op1),
                         *after, cost=cost_of(DV, out))

        def act(out, a, func, *after, **kw):
            return AC.do(lambda e: e.activation(out, a, func, **kw), *after, cost=cost_of(AC, out))

        def copy(q, out, a, *after):
            if q is AC:
                return AC.do(lambda e: e.activation(out, a, ACT.Copy), *after, cost=cost_of(AC, out))
            return q.do(lambda e: e.tensor_copy(out, a), *after, cost=cost_of(q, out, 0.8))

        def mm(out, lhsT, rhs, start, stop, *after, inc=True, tile=False):
            f = lambda e: e.matmul(out, lhsT, rhs, start=start, stop=stop, skip_group_check=True)
            n = max(width(out), 64 if not tile else 20)
            c = n / 2400 if rhs.dtype == F32R else n / 600
            return PE.do(f, *after, cost=c) if inc else PE.raw(f, *after, cost=c)

        def tr(out, in_, *after, inc=True):
            f = lambda e: e.transpose(out, in_, C["ident"])
            return PE.do(f, *after, cost=0.11) if inc else PE.raw(f, *after, cost=0.11)

        def split(hi, lo, src, *after):
            t = copy(DV, hi, src, *after)
            return tt(DV, lo, src, hi.bitcast(F32), ALU.subtract, t)

        l_v, l_c = Line(sem("l_v")), Line(sem("l_c"))
        SP.dma(lambda e: e.dma_start(vec[:, :], vecs), l_v)
        t_vec = SP.dma(lambda e: e.dma_start(cst[:, 0:2, :], consts[:, 0:2, :]), l_v)
        t_x = []
        for i in range(4):
            l_x = Line(sem(f"l_x{i}"))
            t_x += [SP.dma(lambda e, i=i: e.dma_start(x[:, 2 * i:2 * i + 2, :], xT[:, 2 * i:2 * i + 2, :]), l_x)] * 2
        wb = A(38, 2).rearrange("p a b -> p (a b)")
        wbr = arena_r[:, 38:40, :].rearrange("p a b -> p (a b)")
        wb_raw, wb_hi, wb_lo = wb[:, 0:256], wbr[:, 256:512], wbr[:, 512:768]

        def load_rest():
            SP.dma(lambda e: e.dma_start(wb_raw, wba), l_c)
            SP.dma(lambda e: e.dma_start(A(12, 2), cossin), l_c)
            return SP.dma(lambda e: e.dma_start(cst[:, 2:, :], consts[:, 2:, :]), l_c)

        t_idr = copy(DV, ident_r[:, :], C["ident"], t_vec)
        t_pad = DV.do(lambda e: e.memset(pad[:, :, :], 0.0))
        t_eps = DV.do(lambda e: e.memset(eps, EPS))
        AC.raw(lambda e: e.add_instruction(mybir.InstLoadActFuncSet(
            name=nc.get_next_instruction_name(), act_func_set_id=SET_LN_EXP)))

        n_pairs = wstream.shape[0]
        lines = [Line(sem(f"l_w{i}")) for i in range(NRAW)]
        dma_tok, split_tok = {}, {}
        raw_free = [()] * NRAW
        spl_free = [()] * NSPL

        def load_pair(p):
            i = p % NRAW
            dma_tok[p] = SP.dma(lambda e: e.dma_start(raw[:, i, :], wstream[p]), lines[i], raw_free[i])

        split_hi = {}

        def split_pair(p, parts=range(4), half=None):
            if p >= n_pairs:
                return
            i, j = p % NRAW, p % NSPL
            for a in parts:
                c = slice(a * 512, a * 512 + 512)
                hi, lo, w = spl[:, j, 0, c], spl[:, j, 1, c], raw[:, i, c]
                if half != 1:
                    split_hi[a] = copy(AC, hi, w, dma_tok[p], spl_free[j])
                if half != 0:
                    last = tt(DV, lo, w, hi.bitcast(F32), ALU.subtract, split_hi[a])
            if 3 in parts and half != 0:
                split_tok[p] = raw_free[i] = last
                if p + NRAW < n_pairs:
                    load_pair(p + NRAW)

        load_pair(0)
        t_rest = load_rest()
        t_const = (t_vec, t_rest)
        for p in range(1, NRAW):
            load_pair(p)

        class Stream:
            blk = 0

        def block():
            p, b = divmod(Stream.blk, 16)
            if b in (5, 7, 9, 11):
                split_pair(p + 1, [(b - 5) // 2], 0)
            if b in (6, 8, 10, 12):
                split_pair(p + 1, [(b - 6) // 2], 1)
            Stream.blk += 1
            j = p % NSPL
            c = slice(b * 128, b * 128 + 128)
            return spl[:, j, 0, c], spl[:, j, 1, c], split_tok[p], b == 15, j

        lanes = {}
        margin = [float(MARGIN)]

        def spawn(lane, gen):
            lanes.setdefault(lane, Lane()).queue.append(gen)

        class Lane:

            def __init__(self):
                self.queue, self.ready, self.idle = [], 0.0, False

        def advance(lane):
            before = [len(q.items) for q in (PE, DV, AC, PO)]
            for q in (PE, DV, AC, PO):
                q.latest = 0.0
            try:
                next(lane.queue[0])
            except StopIteration:
                lane.queue.pop(0)
            lane.idle = before == [len(q.items) for q in (PE, DV, AC, PO)]
            lane.ready = 0.0 if lane.idle else max(q.latest for q in (DV, AC, PO))
            return not lane.idle

        def step(force=False):
            moved = False
            for name in sorted(lanes, key=lambda n: PRIORITY.get(n[:4], 3)):
                lane = lanes[name]
                if lane.queue and (lane.idle or lane.ready <= PE.clock - margin[0]):
                    moved = advance(lane) or moved
            if force and not moved:
                waiting = [x for x in lanes.values() if x.queue and not x.idle]
                if waiting:
                    advance(min(waiting, key=lambda x: x.ready))

        def drain(*names):
            n = 0
            while any(lanes[k].queue for k in (names or list(lanes)) if k in lanes):
                step(True)
                n += 1
                assert n < 100000

        later = []

        def flush(keep=0):
            while len(later) > keep:
                later.pop(0)()

        class Act_:

            def __init__(self, hi, lo):
                self.hi, self.lo, self.tok = hi, lo, [None] * len(hi)

            def put(self, k, src, *after, then=None):
                t = copy(AC, self.hi[k], src, *after)
                self.tok[k] = None

                def lo():
                    self.tok[k] = tt(DV, self.lo[k], src, self.hi[k].bitcast(F32), ALU.subtract, t)
                    if then:
                        then(self.tok[k])
                later.append(lo)

        def give(slot, *toks):
            slot.free = toks

        main = Ring([psum[0][:, :], psum[1][:, :]])

        def gemm(a, K, done):
            while not main.ready():
                step(True)
            slot, free = main.next()
            PE.wait(free)
            tok = None
            for k in range(K):
                wh, wl, ready, last, j = block()
                f = k == 0
                e = k == K - 1
                if k == 1 or a.tok[k] is None:
                    flush()
                mm(slot.ap, wh, a.hi[k], f, False, ready, a.tok[k], inc=False)
                mm(slot.ap, wh, a.lo[k], False, False, inc=False)
                tok = mm(slot.ap, wl, a.hi[k], False, e, inc=last or e)
                if last:
                    spl_free[j] = tok
                if not e:
                    step()
            done(slot, tok)
            step()

        def gemm2(a, dones):
            while sum(s.free is not None for s in main.slots) < 2:
                step(True)
            outs = [main.next() for _ in dones]
            for k in range(KT):
                while a.tok[k] is None:
                    flush()
                for u, (slot, free) in enumerate(outs):
                    wh, wl, ready, last, j = block()
                    mm(slot.ap, wh, a.hi[k], k == 0, False, ready, a.tok[k], free, inc=False)
                    mm(slot.ap, wh, a.lo[k], False, False, inc=False)
                    tok = mm(slot.ap, wl, a.hi[k], False, k == KT - 1, inc=k == KT - 1)
            spl_free[j] = tok
            for (slot, _), done in zip(outs, dones):
                done(slot, tok)
            step()

        def gemm_tok(a, done):
            flush()
            p, b = divmod(Stream.blk, 16)
            assert b == 0
            j = p % NSPL
            ready = split_tok[p]
            wh = spl[:, j, 0, :].rearrange("p (k n) -> p k n", k=8)
            wl = spl[:, j, 1, :].rearrange("p (k n) -> p k n", k=8)
            for tb in range(4):
                if tb == 1:
                    split_pair(p + 1)
                while not main.ready():
                    step(True)
                slot, free = main.next()
                PE.wait(free)
                c = slice(tb * 128, tb * 128 + 128)
                o = slot.ap[:, 0:256]
                tok = None
                for k in range(8):
                    mm(o, a.hi[k][:, c], wh[:, k, :], k == 0, False, ready, a.tok[k], inc=False)
                    mm(o, a.hi[k][:, c], wl[:, k, :], False, False, inc=False)
                    tok = mm(o, a.lo[k][:, c], wh[:, k, :], False, k == 7, inc=k == 7)
                    if k % 2 == 1 and k < 7:
                        step()
                spl_free[j] = tok
                done(tb, slot, tok)
                step()
            Stream.blk += 16

        def rstd_from(ps, out, n, *after):
            t = act(out, ps, ACT.Ln, *after, scale=1.0 / n, bias=eps)
            return act(out, out, ACT.Exp, t, scale=-0.5), t

        def sigmoid_(buf, src, *after):
            t = act(buf, src, ACT.Exp, *after, scale=-1.0)
            t = act(buf, buf, ACT.Ln, t, bias=1.0)
            return act(buf, buf, ACT.Exp, t, scale=-1.0)

        class SumSq:

            def __init__(self, acc, tmp, quick=False):
                self.acc, self.tmp, self.n, self.t_add, self.t_free = acc, tmp, 0, None, [(), ()]
                self.quick, self.t_rs = quick, None

            def add(self, src, *after):
                if self.n == 0:
                    t = act(self.acc, src, ACT.Square, *after)
                    self.t_add = t
                else:
                    i = self.n % 2
                    t = act(self.tmp[i], src, ACT.Square, *after, self.t_free[i])
                    q = DV if self.quick or self.n == 7 else PO
                    self.t_add = tt(q, self.acc, self.acc, self.tmp[i], ALU.add, t, self.t_add)
                    self.t_free[i] = self.t_add
                self.n += 1
                return t

            def rstd(self, bank, free, out, n, *after):
                t = mm(bank, C["ones"], self.acc, True, True, self.t_add, free)
                return rstd_from(bank, out, n, t, *after)

        def first_norm(a, gain, acc, tmp, rs, bank, srcs_tok, pre):
            sq = SumSq(acc, tmp, True)
            for k in range(KT):
                sq.add(x[:, k, :], srcs_tok[k])
            split_pair(0)
            t_rs, t_rel = sq.rstd(bank.ap, bank.free, rs, 1024, pre)
            bank.free = (t_rel,)
            last = [None, None]
            for k in range(KT):
                b = tmp[k % 2]
                t = stt(b, x[:, k, :], V(gain, k), rs, ALU.mult, ALU.mult, t_rs, srcs_tok[k], last[k % 2])
                a.put(k, b, t, then=lambda t, k=k: last.__setitem__(k % 2, t))
                flush(1)
            flush()

        on_t = sb("on_t", [128, 2, S])

        h = Act_([hh[:, k, :] for k in range(KT)], [hl[:, k, :] for k in range(KT)])
        side = [psum[i][:, :] for i in range(2, 8)]
        nb = Slot(side[0])
        first_norm(h, "norm_pre", A(32), [A(33), A(34)], A(35), nb, t_x, (t_vec, t_eps))
        t_wbs = split(wb_hi, wb_lo, wb_raw, t_const)

        X = [x[:, k, :] for k in range(KT)]
        qT = [A(i) for i in range(8)]
        kT = [A(8), A(9)]
        vtok = A(10, 2).rearrange("p a b -> p (a b)").rearrange("p (t n) -> p t n", t=4)
        cosA, sinA = A(12), A(13)
        ua = [A(16 + i) for i in range(8)]
        aux = Ring([side[1], side[2]])
        rope_tmp = Ring([(A(24), A(25), A(26)), (A(27), A(28), A(29))])
        qw = cols(1)
        t_qw = ts(DV, qw, V("q_norm"), 128.0 ** -0.5, None, ALU.mult, None, t_const)
        t_x_dead = h.tok[KT - 1]

        q_tok = {}

        def rope_gen(key, slot, tok, dst, wcol, ones_m, n, rot_m, cosv, sinv, tmp_ring, aux_ring, after=(), rows=None):
            while not tmp_ring.ready():
                yield
            tmp, tfree = tmp_ring.next()
            t_, sq, rs = tmp.ap
            if rows is None:
                t1 = act(sq, slot.ap, ACT.Square, tok, tfree)
                t2 = act(t_, slot.ap, ACT.Identity, tok, after, scale=wcol)
                slot.free = (t1, t2)
            else:
                t = tt(DV, t_, slot.ap, rows[0], ALU.mult, tok, tfree, rows[1])
                slot.free = (t,)
                t1 = act(sq, t_, ACT.Square, t)
                t2 = act(t_, t_, ACT.Identity, t, after, scale=wcol)
            yield
            b, free = aux_ring.next()
            t3 = mm(b.ap, ones_m, sq, True, True, t1, free)
            t4, t4r = rstd_from(b.ap, rs, n, t3)
            b.free = (t4r,)
            if rows is not None:
                yield
            b2, free = aux_ring.next()
            t5 = mm(b2.ap, rot_m, t_, True, True, t2, free)
            t6 = tt(PO, t_, t_, cosv, ALU.mult, t5, t2, after)
            t7 = tt(DV, sq, b2.ap, sinv, ALU.mult, t5, t3, after)
            b2.free = (t7,)
            yield
            t8 = tt(DV, t_, t_, sq, ALU.add, t6, t7)
            t9 = tt(DV, dst, t_, rs, ALU.mult, t8, t4)
            tmp.free = (t9,)
            q_tok[key] = t9

        def proj_rope(key, dst, wcol):
            def done(slot, tok):
                spawn("rope", rope_gen(key, slot, tok, dst, wcol, C["ones"], 128, C["rot_a"], cosA, sinA,
                                       rope_tmp, aux, (t_const, t_qw)))
            return done

        v_tok = {}

        def v_done(tb, slot, tok):
            t = copy(AC if tb % 2 else DV, vtok[:, tb, :], slot.ap[:, 0:256], tok)
            slot.free = (t,)
            v_tok[tb] = t

        gemm2(h, [proj_rope("k0", kT[0], V("k_norm")), proj_rope("k1", kT[1], V("k_norm"))])
        gemm_tok(h, v_done)

        def g3(c):
            return c.rearrange("p (t n) -> p t n", t=4)

        gcol, beta, neg_eg, edec, graw = (cols(64) for _ in range(5))
        gt0, gt1 = cols(64), cols(64)
        eglast = cols(64)
        bankg, bank5 = Slot(side[3]), Slot(side[5])
        for k in range(KT):
            wh, wl = wb_hi[:, k * 32:k * 32 + 32], wb_lo[:, k * 32:k * 32 + 32]
            mm(bankg.ap[0:32, :], wh, hh[:, k, :], k == 0, False, h.tok[k], t_wbs, inc=False)
            mm(bankg.ap[0:32, :], wl, hh[:, k, :], False, False, inc=False)
            tok = mm(bankg.ap[0:32, :], wh, hl[:, k, :], False, k == 7, inc=k == 7)
        step()
        rows = A(40)[0:32, :]
        t_rows = copy(DV, rows, bankg.ap[0:32, :], tok)
        for tb in range(4):
            f = lambda e, tb=tb: e.transpose(bank5.ap[:, tb * 32:tb * 32 + 32],
                                             rows[:, tb * 128:tb * 128 + 128], C["ident"][0:32, 0:32])
            tok = PE.do(f, t_rows)
        bg = bank5.ap[:, 0:128].rearrange("p (t n) -> p t n", t=4)
        db, da = bg[:, :, 0:16], bg[:, :, 16:32]
        t1 = act(g3(beta), db, ACT.Exp, tok, scale=-1.0)
        t1 = ts(DV, beta, beta, 1.0, None, ALU.add, None, t1)
        t_beta = DV.do(lambda e: e.reciprocal(beta, beta), t1)
        tl = None
        for tb in range(4):
            tl = tt(DV, g3(gt0)[:, tb, :], da[:, tb, :], V("dt_bias", 0, 16), ALU.add, tok, t_const, t1)
        t2 = act(gt1, gt0, ACT.Abs, tl)
        t2 = act(gt1, gt1, ACT.Exp, t2, scale=-1.0)
        t2 = act(gt1, gt1, ACT.Ln, t2, bias=1.0)
        t3 = stt(gt0, gt0, 0.0, gt1, ALU.max, ALU.add, t2)
        alog = cols(16)
        t4 = act(alog, V("a_log", 0, 16), ACT.Exp, t_const)
        for tb in range(4):
            t5 = stt(g3(graw)[:, tb, :], g3(gt0)[:, tb, :], -1.0, alog, ALU.mult, ALU.mult, t3, t4)
        step()
        bankc = Slot(side[4])
        cum = bankc.ap[:, 0:64].rearrange("p (t n) -> p t n", t=4)
        for tb in range(4):
            mm(cum[:, tb, 0:8], C["tri_u"], g3(graw)[:, tb, 0:8], tb == 0, False, t5, inc=False)
            mm(cum[:, tb, 8:16], C["tri_l"], g3(graw)[:, tb, 8:16], False, False, inc=False)
        t6 = mm(bankc.ap[:, 128:192], C["ones"], graw, False, True)
        t_gcol = copy(DV, gcol, bankc.ap[:, 0:64], t6)
        t7 = act(neg_eg, bankc.ap[:, 0:64], ACT.Exp, t6, t_gcol)
        t_neg = ts(DV, neg_eg, neg_eg, -1.0, None, ALU.mult, None, t7)
        t8 = tt(DV, edec, bankc.ap[:, 128:192], gcol, ALU.subtract, t_gcol, t6, t7)
        t_edec = act(edec, edec, ACT.Exp, t8)
        step()
        bankt = Slot(side[3])
        for tb in range(4):
            t9 = tr(bankt.ap[0:16, tb * 128:tb * 128 + 128], g3(gcol)[:, tb, :], t_gcol, t_rows, inc=tb == 3)
        t_gT = split(gTh[:, :], gTl[:, :], bankt.ap[0:16, :], t9)
        gate_tok = (t_gcol, t_beta, t_neg, t_edec, t_gT)
        drain("rope")

        ring_s = Ring([side[3], side[4]])
        ring_t = aux
        ring_o = Ring([side[0], side[5]])
        ring_s.slots[0].free = (t_gT,)
        ring_s.slots[1].free = (t7, t8)
        ring_o.slots[0].free = nb.free
        ring_o.slots[1].free = (t1, tl)
        p_ring = Ring([X[0], X[1], X[2]])
        for s in p_ring.slots:
            s.free = (t_x_dead,)
        pt_ring = Ring([x[:, 3:7, :], A(32, 4)])
        pt_ring.slots[0].free = pt_ring.slots[1].free = (t_x_dead,)
        sil = Ring([A(36), A(37)])
        mx, sm, ri = cols(16), cols(16), cols(16)
        ua_tok = {}
        att_done = {}
        sm_i = [0]

        def gqa_head(hd):
            g = hd // 4
            while f"q{hd}" not in q_tok or not pt_ring.ready():
                yield
            pt, pfree = pt_ring.next()
            tpt = []
            for qb in range(4):
                while not p_ring.ready():
                    yield
                s, free = ring_s.next()
                t = mm(s.ap, qT[hd][:, qb * 128:qb * 128 + 128], kT[g], True, True,
                       free, q_tok[f"q{hd}"], q_tok[f"k{g}"])
                i = sm_i[0] % 16
                sm_i[0] += 1
                m, su, rr = mx[:, i:i + 1], sm[:, i:i + 1], ri[:, i:i + 1]
                tm = DV.do(lambda e, a=s.ap, m=m: e.tensor_reduce(m, a, AX_X, ALU.max, negate=True), t, cost=0.6)
                p, free2 = p_ring.next()
                te = act(p.ap, s.ap, ACT.Exp, tm, free2, bias=m, accum_out=su)
                s.free = (te, tm)
                yield
                tr1 = DV.do(lambda e, su=su, rr=rr: e.reciprocal(rr, su), te)
                tp = ts(DV, p.ap, p.ap, rr, None, ALU.mult, None, tr1)
                yield
                b, free3 = ring_t.next()
                for kb in range(4):
                    t = tr(b.ap[:, kb * 128:kb * 128 + 128], p.ap[:, kb * 128:kb * 128 + 128], tp, free3,
                           inc=kb == 3)
                p.free = (t,)
                tc = copy(DV if qb % 2 else AC, pt.ap[:, :, qb * 128:qb * 128 + 128],
                          b.ap.rearrange("p (k q) -> p k q", k=4), t, pfree)
                b.free = (tc,)
                tpt.append(tc)
                yield
            while not ring_o.ready():
                yield
            o, free = ring_o.next()
            for kb in range(4):
                t = mm(o.ap, vtok[:, kb, g * 128:g * 128 + 128], pt.ap[:, kb, :], kb == 0, kb == 3,
                       tpt, free, v_tok[kb], inc=kb == 3)
            pt.free = (t,)
            while hd not in ua_tok:
                yield
            t = tt(DV, ua[hd], ua[hd], o.ap, ALU.mult, t, ua_tok[hd])
            o.free = (t,)
            att_done[hd] = t

        def att_all(lane):
            for hd in range(lane, 8, 2):
                yield from gqa_head(hd)

        def silu_done(dst, toks, i, after=()):
            def done(slot, tok):
                b, free = sil.next()
                t = sigmoid_(b.ap, slot.ap, tok, free)

                def last():
                    toks[i] = tt(DV, dst, slot.ap, b.ap, ALU.mult, t, after)
                    b.free = slot.free = (toks[i],)
                later.append(last)
            return done

        for lane in range(2):
            spawn(f"att{lane}", att_all(lane))
        for i in range(8):
            gemm(h, KT, proj_rope(f"q{i}", qT[i], qw))
        for i in range(8):
            gemm(h, KT, silu_done(ua[i], ua_tok, i))

        flush()
        drain()
        t_att_last = [att_done[i] for i in range(8)]
        spill = nc.dram_tensor("spill", [128, KT, S], F32).ap()
        l_sp = Line(sem("l_sp"))
        t_spill = SP.dma(lambda e: e.dma_start(spill, arena[:, 16:24, :]), l_sp, t_att_last)
        dead = (t_att_last, t_spill, [s.free for s in p_ring.slots], [s.free for s in pt_ring.slots],
                [s.free for s in rope_tmp.slots], [s.free for s in sil.slots])
        free_tiles = [A(i) for i in range(41)] + X
        it = iter(free_tiles)
        keep = Ring([{k: next(it) for k in ("k", "v", "kt", "X0", "X1", "AT0", "AT1", "qe0", "qe1")}
                     for _ in range(3)])
        n32 = lambda ap: ap.rearrange("p (g n) -> p g n", n=32)
        n64 = lambda ap: ap.rearrange("p (g n) -> p g n", n=64)
        t_zero = None
        sets = []
        for _ in range(2):
            w = {k: next(it) for k in ("D", "G", "TA", "B0", "B1")}
            w["M64"] = w["G"]
            for k in ("hB", "hC0", "hT"):
                t = next(it)
                w[k], w[{"hB": "hM", "hC0": "hC1", "hT": "hX"}[k]] = n32(t[:, 0:256]), n32(t[:, 256:512])
            t_zero = PO.do(lambda e, a=w["TA"]: e.memset(a, 0.0), dead)
            sets.append(w)
        for s in keep.slots:
            for k in ("X0", "X1"):
                t_zero = PO.do(lambda e, a=s.ap[k]: e.memset(a, 0.0), dead)
        work = Ring(sets)
        for s in work.slots:
            s.free = (dead, t_zero)
        acc_ring = Ring([next(it), next(it), next(it)])
        e_ring = Ring([on_t[:, 0, :], on_t[:, 1, :]])
        q_tile = next(it)
        for s in keep.slots + acc_ring.slots + e_ring.slots:
            s.free = dead
        q_free = [dead]
        pads = Ring([pad[:, i, :] for i in range(2)])
        prep_banks = Ring([side[0], side[1], side[2]])
        scan_banks = Ring([side[3], side[4]])
        obank = Slot(side[5])
        for s, t in zip(prep_banks.slots, (ring_o.slots[0].free, ring_t.slots[0].free, ring_t.slots[1].free)):
            s.free = t
        for s, t in zip(scan_banks.slots, (ring_s.slots[0].free, ring_s.slots[1].free)):
            s.free = t
        obank.free = ring_o.slots[1].free
        obank_free = [obank.free]
        conv_in = {}
        prep_done = {}
        dn_tok = {}

        def conv_evict(i):
            def done(slot, tok):
                p, free = pads.next()
                t = copy(AC, p.ap[:, 2:514], slot.ap, tok, free, t_pad)
                slot.free = (t,)
                conv_in[i] = (p, t)
                spawn("conv", conv_gen(i))
            return done

        def conv_gen(i):
            p, t = conv_in[i]
            while not acc_ring.ready() or not e_ring.ready():
                yield
            a, free = acc_ring.next()
            e, efree = e_ring.next()
            w = lambda j: V("conv", i * 5 + j)
            t = ts(DV, a.ap, p.ap[:, 0:512], w(0), None, ALU.mult, None, t, free)
            for j in range(1, 5):
                t = stt(a.ap, p.ap[:, j:j + 512], w(j), a.ap, ALU.mult, ALU.add, t)
                if j in (2, 4):
                    yield
            p.free = (t,)
            t = sigmoid_(e.ap, a.ap, t, efree)
            t = tt(DV, a.ap, a.ap, e.ap, ALU.mult, t)
            hd = i % 8
            if i >= 16:
                e.free = (t,)
                yield
                while not prep_banks.ready():
                    yield
                conv_tr(a.ap, keep_of[hd][0].ap["v"], "v", hd, t)
                a.free = (tr_tok["v", hd][0],)
                return
            if i >= 8:
                while not keep.ready():
                    yield
                keep_of[hd] = keep.next()
            dst, dfree = (q_tile, q_free[0]) if i < 8 else (keep_of[hd][0].ap["k"], keep_of[hd][1])
            ta = act(e.ap, a.ap, ACT.Square, t)
            yield
            while not prep_banks.ready():
                yield
            b, bfree = prep_banks.next()
            tb_ = mm(b.ap, C["ones"], e.ap, True, True, ta, bfree)
            tc, tcr = rstd_from(b.ap, e.ap, 1, tb_)
            b.free = (tcr,)
            if i < 8:
                while hd and hd - 1 not in q_used:
                    yield
                dfree = q_free[0]
            td = stt(dst, a.ap, 128.0 ** -0.5 if i < 8 else 1.0, e.ap, ALU.mult, ALU.mult, tc, t, dfree)
            e.free = a.free = (td,)
            qk_tok[i] = td
            if i >= 8:
                yield
                while not prep_banks.ready():
                    yield
                conv_tr(dst, keep_of[hd][0].ap["kt"], "kt", hd, td)

        def conv_tr(src, dst, name, hd, t):
            b, f = prep_banks.next()
            for c in range(4):
                t = tr(b.ap[:, c * 128:c * 128 + 128], g4(src)[:, c, :], t, f, inc=c == 3)
            tc = copy(AC, dst, b.ap, t, keep_of[hd][1])
            b.free = (tc,)
            tr_tok[name, hd] = (t, tc)

        tr_tok, q_used = {}, {}
        keep_of, qk_tok = {}, {}
        g4 = lambda ap: ap.rearrange("p (c n) -> p c n", c=4)
        bc4 = lambda m: m.unsqueeze(1).to_broadcast([128, 4, 128])

        def prep_gen(hd):
            while hd + 8 not in qk_tok or hd not in qk_tok:
                yield
            kp, kfree = keep_of[hd]
            K = kp.ap
            tq, tk = qk_tok[hd], qk_tok[hd + 8]
            kt_, qt_ = g4(K["k"]), g4(q_tile)
            while not work.ready() or sum(x.free is not None for x in prep_banks.slots) < 3:
                yield
            wslot, lf = work.next()
            W = wslot.ap
            bkk, f = prep_banks.next()
            for c in range(4):
                mm(bkk.ap[:, c * 128:c * 128 + 128], kt_[:, c, :], kt_[:, c, :], c == 0, c == 3, f, tk, inc=False)
            bkq, f = prep_banks.next()
            for c in range(4):
                tkq = mm(bkq.ap[:, c * 128:c * 128 + 128], kt_[:, c, :], qt_[:, c, :], c == 0, c == 3, tq, f,
                         inc=c == 3)
            tX, tB = [None, None], [None, None]
            LD, LG, LB, hB = W["D"], W["G"], (W["B0"], W["B1"]), W["hB"]
            yield
            for d in range(2):
                col = d * 8 + hd
                while not prep_banks.ready():
                    yield
                bg_, f = prep_banks.next()
                one_col = ident_r[0:16, col:col + 1].to_broadcast([16, 128])
                mm(bg_.ap, one_col, gTh[:, :], True, False, f, gate_tok, t_idr, inc=False)
                tg = mm(bg_.ap, one_col, gTl[:, :], False, True)
                t1 = act(LG, bg_.ap, ACT.Exp, tg, lf, tX[0])
                for c in range(4):
                    t2 = ts(DV, g4(LD)[:, c, :], g4(bg_.ap)[:, c, :], g3(gcol)[:, c, col:col + 1], 0.0,
                            ALU.subtract, ALU.min, tg, t1, lf, tX[0])
                bg_.free = (t1, t2)
                edge = 127 if d == 0 else 0
                e0 = (d * 8 + hd) * 4
                t3 = copy(PO, eglast[:, e0:e0 + 4], g4(LG)[:, :, edge], t1)
                t4 = tt(PO, K[f"qe{d}"], q_tile, LG, ALU.mult, t1, tq, kfree)
                t5 = act(LD, LD, ACT.Exp, t2)
                yield
                t6 = tt(PO, g4(LD), g4(LD), bc4(C["tri_u" if d == 0 else "tri_l"]), ALU.mult, t5)
                t7 = tt(DV, K[f"AT{d}"], bkq.ap, LD, ALU.mult, t6, tkq, kfree)
                for c in range(4):
                    t8 = stt(g4(LB[d])[:, c, :], g4(bkk.ap)[:, c, :], g3(beta)[:, c, col:col + 1],
                             g4(LD)[:, c, :], ALU.mult, ALU.mult, t6, tkq, lf)
                tX[d] = (t3, t4, t7, t8)
                for b in range(4):
                    r = slice(32 * b, 32 * b + 32)
                    tB[d] = copy(DV, hB[r, 4 * d:4 * d + 4, :], g4(LB[d])[r, :, r], t8, lf)
                spawn(f"lev{d}", lev_gen(hd, d, W, K, tX[d], tB[d], kfree, lf))
                yield
            q_free[0] = (tX[0], tX[1])
            q_used[hd] = True
            bkk.free = bkq.free = (tX[0], tX[1])
            while (hd, 0) not in lev_done or (hd, 1) not in lev_done:
                yield
            wslot.free = (lev_done[hd, 0], lev_done[hd, 1], tX[0], tX[1])
            prep_done[hd] = (lev_done[hd, 0], lev_done[hd, 1], tX, tk)

        lev_done = {}

        def lev_gen(hd, d, W, K, tX, tB, kfree, lf):
            g0 = 4 * d
            v = {k: W[k][:, g0:g0 + 4, :] for k in ("hB", "hM", "hC0", "hC1", "hT", "hX")}
            hM, hT, hX, hC = v["hM"], v["hT"], v["hX"], (v["hC0"], v["hC1"])
            B, XF = g4(W[f"B{d}"]), g4(K[f"X{d}"])
            TA, M64 = n64(W["TA"])[:, g0:g0 + 4, :], n64(W["M64"])[:, g0:g0 + 4, :]
            flat = lambda ap: ap.rearrange("p g n -> p (g n)")

            def level_mask(s):
                a = 64 * (s % 2) + 32 * d
                return C[("lev01", "lev23", "lev4i")[s // 2]][:, a:a + 32].unsqueeze(1).to_broadcast([128, 4, 32])

            tCs = [tt(PO, hC[s], v["hB"], level_mask(s), ALU.mult, tB, lf) for s in range(2)]
            idc = C["lev4i"][:, 64:96].unsqueeze(1).to_broadcast([128, 4, 32])
            tXc = tt(DV, hX, idc, hC[0], ALU.subtract, tCs[0], lf)
            tTc = DV.do(lambda e: e.transpose(flat(hT), flat(hX)), tXc, lf, cost=0.25)
            for s in range(1, 5):
                yield
                while not prep_banks.ready():
                    yield
                b, f = prep_banks.next()
                bb = n32(b.ap[:, 0:128])
                for g in range(4):
                    for q in range(4):
                        r = slice(32 * q, 32 * q + 32)
                        t = mm(bb[r, g, :], hC[s % 2][r, g, :], hT[r, g, :], True, True, f, tCs[s % 2], tTc,
                               inc=g == 3 and q == 3, tile=True)
                if s < 4:
                    n = (s + 1) % 2
                    tCs[n] = tt(PO, hC[n], v["hB"], level_mask(s + 1), ALU.mult, t if s > 1 else None, tXc)
                tM = copy(AC, hM, bb, t, lf)
                b.free = (tM,)
                yield
                while not prep_banks.ready():
                    yield
                b, f = prep_banks.next()
                bb = n32(b.ap[:, 0:128])
                for g in range(4):
                    for q in range(4):
                        r = slice(32 * q, 32 * q + 32)
                        t = mm(bb[r, g, :], hM[r, g, :], hX[r, g, :], True, True, f, tM, tXc, inc=g == 3 and q == 3,
                               tile=True)
                tXc = tt(DV, hX, hX, bb, ALU.subtract, t)
                b.free = (tXc,)
                tTc = DV.do(lambda e: e.transpose(flat(hT), flat(hX)), tXc, cost=0.25)
            tE = []
            for q in range(4):
                r = slice(32 * q, 32 * q + 32)
                tE.append(copy(AC, XF[r, :, r], hX[r, :, :], tXc, kfree, lf))
            for q in range(2):
                r = slice(64 * d + 32 * q, 64 * d + 32 * q + 32)
                tE.append(copy(DV, TA[r, :, 32 * q:32 * q + 32], hT[r, :, :], tTc, lf))
            yield
            while not prep_banks.ready():
                yield
            b, f = prep_banks.next()
            bb = n32(b.ap[:, 0:128])
            pairs = [tuple(slice(32 * q, 32 * q + 32) for q in (2 * u + d, 2 * u + 1 - d)) for u in range(2)]
            for sr, ds in pairs:
                for c in range(4):
                    t = mm(bb[ds, c, :], B[sr, c, ds], hT[sr, c, :], True, True, f, tTc, tX, inc=c == 3, tile=True)
            for _, ds in pairs:
                tM = copy(AC, hM[ds, :, :], bb[ds, :, :], t)
            b.free = (tM,)
            yield
            while not prep_banks.ready():
                yield
            b, f = prep_banks.next()
            bb = n32(b.ap[:, 0:128])
            for u, (sr, ds) in enumerate(pairs):
                for c in range(4):
                    mm(bb[sr, c, :], hM[ds, c, :], hX[ds, c, :], True, True, f, tM, inc=False, tile=True)
                    if u == d:
                        mm(bb[ds, c, :], hX[ds, c, :], hM[ds, c, :], True, True, inc=False, tile=True)
            t = PE.mark_last()
            for u, (sr, ds) in enumerate(pairs):
                tN = ts(DV, XF[sr, :, ds], bb[sr, :, :], -1.0, None, ALU.mult, None, t, tE)
                if u == d:
                    tN = ts(DV, TA[ds, :, 32 * d:32 * d + 32], bb[ds, :, :], -1.0, None, ALU.mult, None, t, tE)
            b.free = (tN,)
            yield
            while not prep_banks.ready():
                yield
            sr, ds = (slice(0, 64), slice(64, 128)) if d == 0 else (slice(64, 128), slice(0, 64))
            b, f = prep_banks.next()
            bb = n64(b.ap[:, 0:256])
            for c in range(4):
                t = mm(bb[ds, c, :], B[sr, c, ds], TA[sr, c, :], True, True, f, tN, tE, inc=c == 3, tile=True)
            tM = copy(AC, M64[ds, :, :], bb[ds, :, :], t, lf)
            b.free = (tM,)
            yield
            while not prep_banks.ready():
                yield
            b, f = prep_banks.next()
            bb = n64(b.ap[:, 0:256])
            for c in range(4):
                t = mm(bb[sr, c, :], M64[ds, c, :], XF[ds, c, ds], True, True, f, tM, inc=c == 3, tile=True)
            tN = ts(DV, XF[sr, :, ds], bb[sr, :, :], -1.0, None, ALU.mult, None, t)
            b.free = (tN,)
            lev_done[hd, d] = (tN, tE, tTc)

        st = sb("st", [128, 2, 2, 128])
        kdt = sb("kdt", [128, 2, 128])
        rv = sb("rv", [128, 2, 2, 128])
        st_tok = [(), ()]
        rv_free = [(), ()]
        begun, ended, fin_tok = {}, {}, {}

        def scan_gen(hd, d):
            while (hd not in prep_done or ("v", hd) not in tr_tok or (hd and (hd - 1) not in fin_tok)
                   or (hd, d) in begun):
                yield
            K = keep_of[hd][0].ap
            pre = (prep_done[hd], tr_tok["v", hd][1])
            tS, tvn, trd = None, None, rv_free[d]
            col = d * 8 + hd
            r, vn, kd = rv[:, d, 0, :], rv[:, d, 1, :], kdt[:, d, :]
            bank = scan_banks.slots[d]
            work_ap = bank.ap[:, 0:128]
            for s in range(4):
                c = s if d == 0 else 3 - s
                if s < 3:
                    tkd = ts(PO, kd, g4(K["kt"])[:, c, :], g3(edec)[:, c, col:col + 1], None, ALU.mult, None, trd,
                             gate_tok, tr_tok["kt", hd][1])
                rhs, t_r = g4(K["v"])[:, c, :], None
                if s > 0:
                    t = mm(work_ap, g4(K["k"])[:, c, :], st[:, d, s % 2, :], True, True, tS, bank.free)
                    t_r = stt(r, work_ap, g3(neg_eg)[:, c, col:col + 1], rhs, ALU.mult, ALU.add, t, trd, gate_tok)
                    bank.free = (t_r,)
                    rhs = r
                    yield
                t = mm(work_ap, g4(K[f"X{d}"])[:, c, :], rhs, True, True, t_r, bank.free, pre)
                tvn = act(vn, work_ap, ACT.Identity, t, trd, scale=g3(beta)[:, c, col:col + 1])
                bank.free = (tvn,)
                oc = obank.ap[:, c * 128:c * 128 + 128]
                if s > 0:
                    first = hd not in ended
                    ended[hd] = True
                    mm(oc, st[:, d, s % 2, :], g4(K[f"qe{d}"])[:, c, :], first, False, tS, obank_free[0], inc=False)
                yield
                if s < 3:
                    t = mm(work_ap, kd, vn, True, True, tvn, tkd, bank.free)
                    nxt = st[:, d, (s + 1) % 2, :]
                    if s == 0:
                        tS = copy(DV, nxt, work_ap, t, st_tok[d])
                    else:
                        e0 = (d * 8 + hd) * 4 + c
                        tS = stt(nxt, st[:, d, s % 2, :], eglast[:, e0:e0 + 1], work_ap, ALU.mult, ALU.add, t)
                    bank.free = (tS,)
                first = hd not in ended
                ended[hd] = True
                trd = mm(oc, vn, g4(K[f"AT{d}"])[:, c, :], first, False, tvn, obank_free[0])
                if s < 3:
                    yield
            rv_free[d] = st_tok[d] = (trd,)
            begun[hd, d] = trd
            if (hd, 1 - d) in begun:
                spawn("out", out_gen(hd, (trd, begun[hd, 1 - d])))

        def out_gen(hd, to):
            keep_of[hd][0].free = to
            while not acc_ring.ready() or not e_ring.ready():
                yield
            (sa, fa), (sq, fq) = acc_ring.next(), e_ring.next()
            o_, sq_ = sa.ap, sq.ap
            t1 = act(sq_, obank.ap, ACT.Square, to, fq)
            t2 = act(o_, obank.ap, ACT.Identity, to, fa, scale=V("dn_norm"))
            obank_free[0] = (t1, t2)
            fin_tok[hd] = True
            yield
            while not prep_banks.ready():
                yield
            b, f = prep_banks.next()
            t3 = mm(b.ap, C["ones"], sq_, True, True, t1, f)
            t4, t4r = rstd_from(b.ap, sq_, 128, t3)
            b.free = (t4r,)
            t5 = tt(DV, o_, o_, sq_, ALU.mult, t4, t2)
            t6 = SP.dma(lambda e: e.dma_start(spill2[:, hd, :], o_), l_o[hd % 2], t5)
            sa.free, sq.free = (t6,), (t5,)
            dn_tok[hd] = t6

        l_o = [Line(sem("l_o0")), Line(sem("l_o1"))]
        spill2 = nc.dram_tensor("spill2", [128, KT, S], F32).ap()
        for hd in range(8):
            spawn("prep", prep_gen(hd))
            spawn("scan0", scan_gen(hd, 0))
            spawn("scan1", scan_gen(hd, 1))
            for j in (1, 0, 2):
                while not pads.ready():
                    step(True)
                gemm(h, KT, conv_evict(8 * j + hd))

        T = lambda a, n: [A(a + i) for i in range(n)]
        TR = lambda a, n: [R(a + i) for i in range(n)]
        while 5 not in fin_tok:
            step(True)
        assert keep_of[5][0] is keep.slots[2] and keep.slots[2].free is not None
        t_k5 = keep.slots[2].free
        sil = Ring([X[6], X[7]])
        for s in sil.slots:
            s.free = dead
        dzs, dz_tok = T(18, 8), {}
        for m in range(KT):
            gemm(h, KT, silu_done(dzs[m], dz_tok, m, t_k5))
            if m == RELOAD_AT:
                flush()
                while 6 not in fin_tok:
                    step(True)
                assert keep_of[6][0] is keep.slots[0] and work.slots[0].free is not None
                t_k6 = (keep.slots[0].free, prep_done[6])
                t_ua = SP.dma(lambda e: e.dma_start(arena[:, 0:8, :], spill), l_sp, t_k6)
        flush()
        ua, ud = T(0, 8), T(9, 8)
        yA, yD = Act_(TR(0, 8), TR(27, 8)), Act_(TR(9, 8), TR(18, 8))
        halves = Ring([R(8), R(26)])
        halves.slots[0].free, halves.slots[1].free = t_k6, t_k5

        def split_in_place(a, src, k, *after):
            b, free = halves.next()
            t = DV.do(lambda e: e.tensor_copy(b.ap, src[k]), free, *after)
            t = tt(DV, a.lo[k], src[k], b.ap.bitcast(F32), ALU.subtract, t)
            a.tok[k] = copy(AC, a.hi[k], b.ap.bitcast(F32), t)
            b.free = (a.tok[k],)

        for k in range(KT):
            split_in_place(yA, ua, k, t_k6, t_k5, t_ua)

        drain()

        t_all = [list(dn_tok.values()), prep_done[7], prep_done[6], rv_free, [s.free for s in keep.slots]]
        l_ud = Line(sem("l_ud"))
        t_ud = SP.dma(lambda e: e.dma_start(arena[:, 9:17, :], spill2), l_ud, t_all)
        gates = Ring([A(35), A(36), A(37)])
        prod = Ring([A(38), A(39)])
        gate_of = {}

        def gate_done(slot, tok):
            b, free = gates.next()
            gate_of["g"] = (b, sigmoid_(b.ap, slot.ap, tok, free, t_all))
            slot.free = (gate_of["g"][1],)

        mix_a = {}

        def y_att_done(m):
            def done(slot, tok):
                b, t = gate_of["g"]
                mix_a[m] = tt(DV, X[m], slot.ap, b.ap, ALU.mult, tok, t, t_all)
                b.free = slot.free = (mix_a[m],)
            return done

        for m in range(KT):
            gemm(h, KT, gate_done)
            gemm(yA, KT, y_att_done(m))
            t = tt(DV, ud[m], ud[m], dzs[m], ALU.mult, dz_tok[m], t_ud)
            split_in_place(yD, ud, m, t)
        t_ya = main.slots[main.i % 2].free
        mix = Act_(TR(0, 8), TR(27, 8))

        def y_dn_done(m):
            def done(slot, tok):
                b, t = gate_of["g"]
                p, free = prod.next()
                t = tt(DV, p.ap, slot.ap, b.ap, ALU.mult, tok, t, free, t_all)
                b.free = slot.free = (t,)
                t = tt(DV, X[m], X[m], p.ap, ALU.add, t, mix_a[m])
                mix.put(m, X[m], t, t_ya, then=lambda t: give(p, t))
            return done

        for m in range(KT):
            gemm(h, KT, gate_done)
            gemm(yD, KT, y_dn_done(m))
        flush()
        t_h_dead = gate_of["g"][1]
        t_mix = [mix.tok[m] for m in range(KT)]
        t_yd = main.slots[main.i % 2].free
        ones_bank = Slot(side[0])
        ones_bank.free = t_all

        l_x = Line(sem("l_x"))
        t_x = SP.dma(lambda e: e.dma_start(x[:, :, :], xT), l_x, t_mix)
        pin = A(18, 2)
        l_p = Line(sem("l_p"))
        t_p = SP.dma(lambda e: e.dma_start(pin, pT), l_p, t_yd)
        pa = Act_(TR(20, 2), TR(22, 2))
        y = T(9, 8)
        sq_bufs = (A(35), [A(36), A(37)], A(40))
        sq = SumSq(sq_bufs[0], sq_bufs[1])
        sq.t_free = [(gates.slots[0].free, gates.slots[1].free, gates.slots[2].free)] * 2
        y_tok = {}

        def y_done(m):
            def done(slot, tok):
                y_tok[m] = copy(DV, y[m], slot.ap, tok, t_yd, *sq.t_free)
                sq.add(y[m], y_tok[m])
                slot.free = (y_tok[m],)
            return done

        for m in range(KT):
            gemm(mix, KT, y_done(m))
        for k in range(2):
            pa.put(k, pin[:, k, :], t_p)
        flush()
        t_mixread = y_tok[KT - 1]
        e_ = T(0, 8)
        e_tok = {}

        def e_done(m):
            def done(slot, tok):
                e_tok[m] = copy(AC, e_[m], slot.ap, tok, t_mixread)
                slot.free = (e_tok[m],)
            return done

        x_tok = [None] * KT
        for m in range(KT):
            gemm(pa, 2, e_done(m))
            if m == 1:
                rs_mix = sq.rstd(ones_bank.ap, ones_bank.free, sq_bufs[2], 1024)
                ones_bank.free = (rs_mix[1],)

        def add_normed(src, src_tok, t_rs, gain, each):
            rs = sq_bufs[2]
            for i in range(KT + 1):
                if i < KT:
                    t = stt(src[i], src[i], V(gain, i), rs, ALU.mult, ALU.mult, t_rs, src_tok[i])
                    x_tok[i] = tt(PO, x[:, i, :], x[:, i, :], src[i], ALU.add, t, t_x, x_tok[i])
                flush()
                if i > 0:
                    each(i - 1, x_tok[i - 1])
            flush()

        add_normed(y, y_tok, rs_mix[0], "norm_post", lambda k, t: h.put(k, x[:, k, :], t, t_h_dead))
        sq2 = SumSq(sq_bufs[0], sq_bufs[1])
        sq2.t_free = [(x_tok[KT - 1],)] * 2
        gates2 = Ring([A(38), A(39)])
        gates2.slots[0].free = gates2.slots[1].free = (x_tok[KT - 1],)
        z_tok = {}

        def z_done(m):
            def done(slot, tok):
                b, free = gates2.next()
                t = sigmoid_(b.ap, slot.ap, tok, free)
                slot.free = (t,)

                def last():
                    z_tok[m] = tt(DV, y[m], b.ap, e_[m], ALU.mult, t, e_tok[m], x_tok[m], *sq2.t_free)
                    b.free = (z_tok[m],)
                    sq2.add(y[m], z_tok[m])
                later.append(last)
            return done

        gemm2(h, [z_done(0), z_done(1)])
        for m in range(2, KT):
            gemm(h, KT, z_done(m))
        nsq = {}
        scaled = Ring([on_t[:, 0, :], on_t[:, 1, :]])

        def new_norm(gain, after):
            nsq["s"] = SumSq(sq_bufs[0], sq_bufs[1])
            nsq["s"].t_free = [after] * 2
            nsq["first"], nsq["gain"], nsq["rs"] = after, gain, sq_bufs[2]
            for s_ in scaled.slots:
                s_.free = after

        def feed_norm(k, t, square=True):
            if square:
                nsq["s"].add(x[:, k, :], t, nsq["first"])
            b, free = scaled.next()
            t = ts(DV, b.ap, x[:, k, :], V(nsq["gain"], k), None, ALU.mult, None, t, free)
            h.put(k, b.ap, t, nsq["first"], then=lambda t: give(b, t))

        def close_norm(bank):
            t, t_rel = nsq["s"].rstd(bank.ap, bank.free, nsq["rs"], 1024, nsq["first"])
            bank.free = (bank.free, t_rel)
            return nsq["rs"], t

        def norm_columns(out):
            while not main.ready():
                step(True)
            b, free = main.next()
            for tb in range(4):
                t = mm(b.ap[:, tb:tb + 1], nsq["s"].acc[:, tb * 128:tb * 128 + 128], C["ones"][:, 0:1], tb == 0,
                       tb == 3, nsq["s"].t_add, free, inc=tb == 3)
            t, t_rel = rstd_from(b.ap[:, 0:4], out, 1024, t)
            b.free = (t_rel,)
            return t

        def after_rstd(k, t):
            if k == 0:
                new_norm("attn0", (t_gate, t))
                nsq["s"].quick = True
            feed_norm(k, t, False)

        flush()
        margin[0] = 0.0
        t_gate = (z_tok[KT - 1], Tok(PE.sem, PE.n))
        rs_ple = sq2.rstd(ones_bank.ap, ones_bank.free, sq_bufs[2], 1024)
        ones_bank.free = (rs_ple[1],)
        add_normed(y, z_tok, rs_ple[0], "ple_norm", after_rstd)
        for k in range(KT):
            nsq["s"].add(x[:, k, :], x_tok[k], nsq["first"])

        rs_col = cols(4)

        def vproj(a, dst, toks, after):
            t_col = norm_columns(rs_col)
            for j in range(4):
                def done(tb, slot, tok, j=j):
                    o, c = dst[:, tb, j * 256:j * 256 + 256], rs_col[:, tb:tb + 1]
                    if tb % 2:
                        t = act(o, slot.ap[:, 0:256], ACT.Identity, tok, after, t_col, scale=c)
                    else:
                        t = ts(DV, o, slot.ap[:, 0:256], c, None, ALU.mult, None, tok, after, t_col)
                    slot.free = (t,)
                    toks[tb, j] = t
                gemm_tok(a, done)

        def stage_end():
            return (Tok(DV.sem, DV.n), Tok(AC.sem, AC.n), Tok(PO.sem, PO.n), Tok(PE.sem, PE.n))

        v8 = arena[:, 0:8, :].rearrange("p a b -> p (a b)").rearrange("p (t n) -> p t n", t=4)
        o8 = T(8, 8)

        cos2, sin2 = A(37), A(38)
        t_trig = []

        def trig_gen():
            pi_, pf, kk = A(32).bitcast(I32), A(33), A(34)
            t = stage_end()
            l_pos = Line(sem("l_pos"))
            t_pos = SP.dma(lambda e: e.dma_start(pi_, pos), l_pos, t)
            for _ in range(12):
                yield
            t = copy(DV, pf, pi_, t_pos, t)
            t_ang = ts(DV, pf, pf, V("invf"), None, ALU.mult, None, t)
            ts_ = ()
            for quarter, kq, dst in ((0.0, kk, sin2), (0.25, A(35), cos2)):
                t = ts(DV, kq, pf, 1.0 / TWO_PI, quarter, ALU.mult, ALU.add, t_ang)
                t = ts(DV, kq, kq, MAGIC, None, ALU.add, None, t)
                yield
                t = ts(DV, kq, kq, MAGIC, None, ALU.subtract, None, t)
                t = stt(dst, kq, -PI_A, pf, ALU.mult, ALU.add, t)
                yield
                t = stt(dst, kq, -PI_B, dst, ALU.mult, ALU.add, t)
                t = stt(dst, kq, -PI_C, dst, ALU.mult, ALU.add, t)
                yield
                if quarter:
                    t = ts(DV, dst, dst, math.pi / 2, None, ALU.add, None, t)
                t = ts(DV, dst, dst, 3.141592, -3.141592, ALU.min, ALU.max, t)
                yield
                ts_ = (ts_, t)
            act(sin2, sin2, ACT.Sin, ts_)
            t_trig.append(act(cos2, cos2, ACT.Sin))

        def out_proj(a, gain):
            new_norm(gain, stage_end())

            def done(m):
                def f(slot, tok):
                    x_tok[m] = tt(DV, x[:, m, :], x[:, m, :], slot.ap, ALU.add, tok, x_tok[m])
                    slot.free = (x_tok[m],)
                    feed_norm(m, x_tok[m])
                return f
            for m in range(KT):
                gemm(a, KT, done(m))
            flush()

        def ffn(i):
            nonlocal sq_bufs
            t0 = stage_end()
            ones_bank.free = t0
            rs = []
            f = Act_(TR(0, FFN_HALF), TR(FFN_HALF, FFN_HALF))
            sl = Ring([A(22), A(23)])
            pr = Ring([A(24), A(25)])
            cur = {}

            def g_done(slot, tok):
                if not rs:
                    rs.extend(close_norm(ones_bank))
                b, free = sl.next()
                t = tt(DV, b.ap, slot.ap, rs[0], ALU.mult, tok, free, t0, rs[1])
                slot.free = (t,)
                cur["g"] = (b, act(b.ap, b.ap, ACT.Silu, t))

            def u_done(k, after):
                def done(slot, tok):
                    b, t = cur["g"]
                    p, free = pr.next()
                    t1 = tt(DV, p.ap, slot.ap, rs[0], ALU.mult, tok, free, t0, rs[1])
                    slot.free = (t1,)
                    t = tt(DV, p.ap, p.ap, b.ap, ALU.mult, t, t1)
                    b.free = (t,)
                    f.put(k, p.ap, t, after, t0, then=lambda t: give(p, t))
                return done

            after = ()
            for half in range(2):
                for k in range(FFN_HALF):
                    gemm(h, KT, g_done)
                    gemm(h, KT, u_done(k, after))
                if half and i == 0:
                    sq_bufs = (A(39), [A(27), A(28)], A(40))
                    new_norm("attn1", stage_end())

                def d_done(m, half=half):
                    def done(slot, tok):
                        x_tok[m] = tt(DV, x[:, m, :], x[:, m, :], slot.ap, ALU.add, tok, x_tok[m])
                        slot.free = (x_tok[m],)
                        if half and i == 0:
                            feed_norm(m, x_tok[m])
                        if half and i == 1:
                            SP.dma(lambda e: e.dma_start(outT[:, m, :], x[:, m, :]), l_out, x_tok[m])
                    return done
                for m in range(KT):
                    gemm(f, FFN_HALF, d_done(m))
                flush()
                after = (x_tok[KT - 1],)

        def load_ln_exp():
            AC.raw(lambda e: e.add_instruction(mybir.InstLoadActFuncSet(
                name=nc.get_next_instruction_name(), act_func_set_id=SET_LN_EXP)))

        l_out = Line(sem("l_out"))

        t0 = stage_end()
        vt_tok = {}
        qk = Ring([(A(16), A(17)), (A(18), A(19))])
        sp_lane = []
        for b in range(2):
            base = 20 + 6 * b
            sp_lane.append({"e": Ring([A(base)]), "sp": Ring([A(base + 1), A(base + 2)]), "sum": Ring([A(base + 3)]),
                            "w": Ring([A(base + 4), A(base + 5)]),
                            "z": Ring([side[3 * b], side[3 * b + 1]]), "o": Ring([side[3 * b + 2]])})
            for r in sp_lane[b].values():
                for s in r.slots:
                    s.free = t0
        for s in qk.slots:
            s.free = t0
        qk_of, heads_left = {}, {}
        rs_a = []

        def stick_head(m, b):
            R = sp_lane[b]
            while m not in qk_of:
                yield
            slot, tq, tk = qk_of[m]
            q_, k_ = slot.ap[0][64 * b:64 * b + 64, :], slot.ap[1][64 * b:64 * b + 64, :]
            o, ofree = R["o"].next()
            su, sfree = R["sum"].next()
            tsum = sfree
            t_z = None
            for kb in (3, 2, 1, 0):
                n = S - 128 * kb
                z, zf = R["z"].next()
                t_z = mm(z.ap[:, 0:n], k_[:, kb * 128:kb * 128 + 128], q_[:, kb * 128:S], True, False, tq, tk, zf)
                e, ef = R["e"].next()
                ea, za = e.ap[:, 0:n], z.ap[:, 0:n]
                t = act(ea, za, ACT.Abs, t_z, ef)
                t = act(ea, ea, ACT.Exp, t, scale=-1.0)
                t = act(ea, ea, ACT.Ln, t, bias=1.0)
                sp, spf = R["sp"].next()
                t1 = stt(sp.ap[:, 0:n], za, 0.0, ea, ALU.max, ALU.add, t, spf)
                e.free = (t1,)
                t1 = tt(PO, sp.ap[:, 0:128], sp.ap[:, 0:128], C["strict_u"], ALU.mult, t1)
                yield
                mm(z.ap[:, 0:128], C["ident"], C["neg_ge"], False, False, t1, inc=False)
                t2 = mm(za, C["neg_tri_l"], sp.ap[:, 0:n], False, kb == 3)
                if kb < 3:
                    t2 = mm(z.ap[:, 128:n], C["neg_ones"], su.ap[:, kb * 128 + 128:S], False, True, tsum)
                    if kb:
                        t3 = tt(PO, su.ap[:, kb * 128 + 128:S], su.ap[:, kb * 128 + 128:S], sp.ap[:, 128:n],
                                ALU.add, t2)
                if kb:
                    tsum = copy(PO, su.ap[:, kb * 128:kb * 128 + 128], sp.ap[:, 0:128], t1, sfree)
                w, wf = R["w"].next()
                tw = act(w.ap[:, 0:n], za, ACT.Exp, t2, wf)
                z.free = (tw,)
                sp.free = (t2, tsum)
                yield
                while (kb, m // 2) not in vt_tok:
                    yield
                c = slice(m * 128, m * 128 + 128)
                t4 = mm(o.ap[:, kb * 128:S], v8[:, kb, c], w.ap[:, 0:n], kb == 3, kb == 0, tw,
                        vt_tok[kb, m // 2], ofree)
                w.free = (t4,)
            su.free = (t2, tsum)
            r = slice(64 * b, 64 * b + 64)
            t = copy(DV, o8[m][r, :], o.ap[r, :], t4, t0)
            o.free = (t,)
            heads_left[m] = heads_left.get(m, ()) + (t,)
            if len(heads_left[m]) == 2:
                slot.free = heads_left[m] + (t_z,)
            yield

        for m in range(8):
            for b in range(2):
                spawn(f"stick{b}", stick_head(m, b))
        for m in range(8):
            while not qk.ready():
                step(True)
            slot_, free_ = qk.next()
            tq_ = {}

            def q_done(bk, tok):
                if not rs_a:
                    zs = sp_lane[0]["z"].slots[0]
                    rs_a.extend(close_norm(zs))
                tq_["q"] = stt(slot_.ap[0], bk.ap, 0.125, rs_a[0], ALU.mult, ALU.mult, tok, free_, rs_a[1])
                bk.free = (tq_["q"],)

            def k_done(bk, tok):
                tq_["k"] = tt(DV, slot_.ap[1], bk.ap, rs_a[0], ALU.mult, tok, free_, rs_a[1])
                bk.free = (tq_["k"],)

            if m == 0:
                gemm2(h, [q_done, k_done])
            else:
                gemm(h, KT, q_done)
                gemm(h, KT, k_done)
            qk_of[m] = (slot_, tq_["q"], tq_["k"])
            if m == 0:
                vproj(h, v8, vt_tok, t0)
        drain()
        oA = Act_(TR(8, 8), TR(32, 8))
        halves = Ring([R(20), R(21)])
        t0 = stage_end()
        halves.slots[0].free = halves.slots[1].free = t0
        for k in range(KT):
            split_in_place(oA, o8, k, heads_left[k])
        sq_bufs = (A(26), [A(27), A(28)], A(29))
        out_proj(oA, "ffn0")
        spawn("trig", trig_gen())
        ffn(0)
        drain("trig")
        load_ln_exp()

        t0 = stage_end()
        l1, l2 = cols(1), cols(1)
        kk = A(34)
        t = DV.do(lambda e: e.tensor_tensor_reduce(kk[:, 0:64], V("lq1", 0, 64), V("lk1", 0, 64), 1.0, 0.0, ALU.mult,
                                                   ALU.add, l1), t0)
        t1 = DV.do(lambda e: e.tensor_tensor_reduce(kk[:, 64:128], V("lq2", 0, 64), V("lk2", 0, 64), 1.0, 0.0,
                                                    ALU.mult, ALU.add, l2), t0)
        ta_ = act(l1, l1, ACT.Exp, t)
        tb_ = act(l2, l2, ACT.Exp, t1)
        t = tt(DV, lam_n, l2, l1, ALU.subtract, ta_, tb_)
        t_lam = ts(DV, lam_n, lam_n, LAM_INIT, None, ALU.subtract, None, t)
        q2w, subw = cols(1), cols(1)
        t_q2w = ts(DV, q2w, V("q2"), 0.125, None, ALU.mult, None)
        t_subw = ts(DV, subw, V("sub_norm"), 1.0 - LAM_INIT, None, ALU.mult, None)

        vt_tok = {}
        qk = Ring([(A(16), A(17)), (A(18), A(19)), (A(23), A(24))])
        rope_tmp = Ring([(A(20), A(21), A(22))])
        pp = Ring([(A(25), A(26)), (A(27), A(28))])
        at_ring = Ring([A(29, 4), A(33, 4)])
        aux = Ring([side[0]])
        sbk = Ring([side[1], side[2], side[3]])
        tbk = Ring([side[4]])
        obk = Ring([side[5]])
        onr = Ring([(on_t[:, 0, :], on_t[:, 1, :])])
        for rg in (qk, rope_tmp, pp, at_ring, aux, sbk, tbk, obk, onr):
            for s in rg.slots:
                s.free = t0
        q_tok.clear()
        o_tok = {}
        cnt = [0]
        rs_b = []
        oB = Act_(TR(8, 8), TR(33, 7) + [R(30)])

        def diff_head(m):
            while ("q", m) not in q_tok or ("k", m) not in q_tok:
                yield
            slot = qk_of[m]
            q_, k_ = slot.ap
            while not at_ring.ready():
                yield
            at, atf = at_ring.next()
            for qb in range(4):
                n = 128 * qb + 128
                while not pp.ready():
                    yield
                pr_, prf = pp.next()
                tp = [None, None]
                ss = []
                for j in range(2):
                    b, f = sbk.next()
                    r = slice(64 * j, 64 * j + 64)
                    mm(b.ap[:, 0:n], q_[r, qb * 128:n], k_[r, 0:n], True, False, f, q_tok["q", m], q_tok["k", m],
                       inc=False)
                    t = mm(b.ap[:, n - 64:n], C["ident"], C["neg64"][:, 0:64], False, True)
                    i = cnt[0] % 16
                    cnt[0] += 1
                    mc, sc, rc = mx[:, i:i + 1], sm[:, i:i + 1], ri[:, i:i + 1]
                    tm = DV.do(lambda e, a=b.ap[:, 0:n], mc=mc: e.tensor_reduce(mc, a, AX_X, ALU.max, negate=True), t,
                               cost=0.08 + n / 1000)
                    te = act(pr_.ap[j][:, 0:n], b.ap[:, 0:n], ACT.Exp, tm, prf, bias=mc, accum_out=sc)
                    b.free = (te, tm)
                    yield
                    trr = DV.do(lambda e, sc=sc, rc=rc: e.reciprocal(rc, sc), te)
                    if j:
                        trr = ts(DV, rc, rc, lam_n, None, ALU.mult, None, trr, t_lam)
                    ss.append((rc, trr, te))
                p1, p2 = pr_.ap[0][:, 0:n], pr_.ap[1][:, 0:n]
                t = ts(DV, p1, p1, ss[0][0], None, ALU.mult, None, ss[0][1])
                t = stt(p1, p2, ss[1][0], p1, ALU.mult, ALU.add, t, ss[1][1])
                yield
                b, f = tbk.next()
                for kb in range(qb + 1):
                    t2 = tr(b.ap[:, kb * 128:kb * 128 + 128], p1[:, kb * 128:kb * 128 + 128], t, f, inc=kb == qb)
                pr_.free = (t2,)
                ta = copy(AC if qb % 2 else DV, at.ap[:, 0:qb + 1, qb * 128:n],
                          b.ap[:, 0:n].rearrange("p (k q) -> p k q", q=128), t2, atf)
                b.free = (ta,)
                o_tok[m, qb] = ta
                yield
            slot.free = (t2, ta)
            while (3, m // 2) not in vt_tok or not obk.ready():
                yield
            o, f = obk.next()
            for kb in range(4):
                t = mm(o.ap[:, kb * 128:S], v8[:, kb, m * 128:m * 128 + 128], at.ap[:, kb, kb * 128:S], kb == 0,
                       kb == 3, f, [o_tok[m, qb] for qb in range(4)], vt_tok[kb, m // 2], inc=kb == 3)
            at.free = (t,)
            while not onr.ready():
                yield
            tn, tf = onr.next()
            t1 = act(tn.ap[1], o.ap, ACT.Square, t, tf)
            t2 = act(o8[m], o.ap, ACT.Identity, t, t_subw, scale=subw)
            o.free = (t1, t2)
            yield
            b, f = tbk.next()
            t3 = mm(b.ap, C["ones"], tn.ap[1], True, True, t1, f)
            t4, t4r = rstd_from(b.ap, tn.ap[1], 128, t3)
            b.free = (t4r,)
            yield
            t = tt(DV, o8[m], o8[m], tn.ap[1], ALU.mult, t2, t4)
            tn.free = (t,)
            o_tok[m] = t

        for m in range(8):
            spawn(f"diff{m % 2}", diff_head(m))
        qk_of = {}
        for m in range(8):
            while not qk.ready():
                step(True)
            slot_, free_ = qk.next()
            qk_of[m] = slot_
            for nm, wc, dst in (("q", q2w, slot_.ap[0]), ("k", V("k2"), slot_.ap[1])):
                def done(bk, tok, nm=nm, wc=wc, dst=dst, free_=free_, m=m):
                    if not rs_b:
                        rs_b.extend(close_norm(aux.slots[0]))
                    spawn("rope", rope_gen((nm, m), bk, tok, dst, wc, C["blk64"], 64, C["rot_b"], cos2, sin2,
                                           rope_tmp, aux, (t_trig, t_q2w, free_), rs_b))
                while not main.ready():
                    step(True)
                gemm(h, KT, done)
            if m == 0:
                while not main.ready():
                    step(True)
                vproj(h, v8, vt_tok, t0)
        drain()
        halves = Ring([R(20), R(21)])
        t0 = stage_end()
        halves.slots[0].free = halves.slots[1].free = t0
        for k in range(KT):
            split_in_place(oB, o8, k, o_tok[k], t0)
        sq_bufs = (A(26), [A(27), A(28)], A(29))
        out_proj(oB, "ffn1")
        ffn(1)
        SP.wait(Tok(l_out.sem, l_out.n))

        block_ = ctx.enter_context(nc.Block())
        block_.sync(SP.emit)
        block_.tensor(PE.emit)
        block_.vector(DV.emit)
        block_.scalar(AC.emit)
        block_.gpsimd(PO.emit)


def shape_constants():
    i = np.arange(128)
    one = lambda m: m.astype(np.float32)
    r, c = i[:, None], i[None, :]
    m = {"ident": one(r == c), "ones": np.ones((128, 128), np.float32), "blk64": one(r // 64 == c // 64),
         "rot_a": one((c == r + 1) & (r % 2 == 0)) - one((r == c + 1) & (c % 2 == 0)),
         "rot_b": one((c == r + 8) & (r % 64 < 8)) - one((r == c + 8) & (c % 64 < 8)),
         "tri_u": one(r <= c), "tri_l": one(r >= c), "neg_tri_l": -one(r >= c),
         "neg_ones": -np.ones((128, 128), np.float32), "strict_u": one(r < c), "neg_ge": -1e30 * one(r >= c),
         "neg64": -1e30 * one((r < 64) & (c < 64))}
    lev = []
    for s in range(5):
        w = 1 << s
        f = one((r // (2 * w) == c // (2 * w)) & (r % (2 * w) < w) & (c % (2 * w) >= w))[:32, :32]
        lev.append(np.tile(np.concatenate([f, f.T], axis=1), (4, 1)))
    lev.append(np.tile(np.concatenate([np.eye(32), np.zeros((32, 32))], axis=1).astype(np.float32), (4, 1)))
    for n, j in (("lev01", 0), ("lev23", 2), ("lev4i", 4)):
        m[n] = np.concatenate([lev[j], lev[j + 1]], axis=1)
    cst = np.stack([m[n].astype(np.float32) for n in CONST_NAMES], axis=1)
    t = np.arange(S)
    inv = (np.float32(10000.0) ** (-np.arange(32, dtype=np.float32) / np.float32(32))).astype(np.float32)
    ang = np.concatenate([(t // 64).astype(np.float32)[:, None] * inv, (t % 64).astype(np.float32)[:, None] * inv], 1)
    cs = np.stack([np.repeat(np.cos(ang), 2, axis=1).T, np.repeat(np.sin(ang), 2, axis=1).T], axis=1)
    inv2 = np.zeros((128, 1), np.float32)
    f2 = (np.float32(500000.0) ** (-np.arange(0, 16, 2, dtype=np.float32) / np.float32(16))).astype(np.float32)
    for b in (0, 8, 64, 72):
        inv2[b:b + 8, 0] = f2
    return np.ascontiguousarray(cst), np.ascontiguousarray(cs.astype(np.float32)), inv2


def lay_out(a):
    out = []
    blocks = []

    def fm(w, c0, n=1, k0=0, k1=None):
        k1 = w.shape[0] // 128 if k1 is None else k1
        for m in range(n):
            for k in range(k0, k1):
                blocks.append(w[k * 128:k * 128 + 128, c0 + m * 128:c0 + m * 128 + 128])
                if len(blocks) == 16:
                    out.append(np.concatenate(blocks, axis=1))
                    blocks.clear()

    def fm2(w, c0, w1, c1):
        for k in range(8):
            fm(w, c0, 1, k, k + 1)
            fm(w1, c1, 1, k, k + 1)

    def tm(w, c0, n):
        assert not blocks
        for j in range(n):
            out.append(w[:, c0 + j * 256:c0 + j * 256 + 256].reshape(8, 128, 256).transpose(1, 0, 2).reshape(128, 2048))

    w = a["w_in"][0]
    fm2(w, 1024, w, 1152)
    tm(w, 1280, 1)
    fm(w, 0, 8)
    fm(w, 1536, 8)
    for hd in range(8):
        for j in (1, 0, 2):
            fm(w, 2560 + 1024 * j + 128 * hd)
    fm(w, 5664, 8)
    for m in range(8):
        fm(w, 6688 + 128 * m)
        fm(a["w_br_att"][0], 128 * m)
    for m in range(8):
        fm(w, 7712 + 128 * m)
        fm(a["w_br_dn"][0], 128 * m)
    fm(a["w_out"][0], 0, 8)
    fm(a["w_ple_proj"][0], 0, 8)
    fm2(a["w_ple_gate"][0], 0, a["w_ple_gate"][0], 128)
    fm(a["w_ple_gate"][0], 256, 6)
    for i in range(2):
        w = a["w_in_2"][i]
        for m in range(8):
            if m == 0 and i == 0:
                fm2(w, 0, w, 1024)
            else:
                fm(w, 128 * m)
                fm(w, 1024 + 128 * m)
            if m == 0:
                tm(w, 2048, 4)
        fm(a["w_out_2"][i], 0, 8)
        for half in range(2):
            for k in range(FFN_HALF * half, FFN_HALF * half + FFN_HALF):
                fm(a["w_gate_2"][i], 128 * k)
                fm(a["w_up_2"][i], 128 * k)
            for m in range(8):
                fm(a["w_down_2"][i], 128 * m, 1, FFN_HALF * half, FFN_HALF * half + FFN_HALF)
    assert not blocks
    return np.stack(out)


def vectors(a, inv2):
    v = np.zeros((128, NVEC), np.float32)

    def put(name, arr):
        s, n = VECS[name]
        v[:, s:s + n] = arr

    col = lambda w: w.reshape(8, 128).T
    for name, arr in (("norm_pre", a["norm_pre"][0]), ("norm_post", a["norm_post"][0]), ("ple_norm", a["ple_norm"][0]),
                      ("attn0", a["attn_norm_2"][0]), ("attn1", a["attn_norm_2"][1]), ("ffn0", a["ffn_norm_2"][0]),
                      ("ffn1", a["ffn_norm_2"][1])):
        put(name, col(arr))
    for name, key in (("q_norm", "q_norm"), ("k_norm", "k_norm"), ("dn_norm", "dn_norm"), ("sub_norm", "sub_norm_2")):
        put(name, a[key][0][:, None])
    for name, key in (("q2", "q_norm_2"), ("k2", "k_norm_2")):
        put(name, np.concatenate([a[key][0], a[key][0]])[:, None])
    put("conv", a["conv_w"][0].reshape(5, 24, 128).transpose(2, 1, 0).reshape(128, 120))
    put("a_log", a["a_log"][0].reshape(1, 16))
    put("dt_bias", a["dt_bias"][0].reshape(1, 16))
    for name, key in (("lq1", "lambda_q1_2"), ("lk1", "lambda_k1_2"), ("lq2", "lambda_q2_2"), ("lk2", "lambda_k2_2")):
        put(name, a[key][0][None, :])
    put("invf", inv2)
    return v


def feature_major(m):
    n = m.shape[1] // 128
    return np.ascontiguousarray(m.T.reshape(n, 128, m.shape[0]).transpose(1, 0, 2))


def kernel(**inputs):
    import concourse.bacc as _bacc
    from concourse.bass_utils import run_bass_kernel_spmd as _run

    a = {k: np.asarray(v) for k, v in inputs.items()}
    cst, cossin, inv2 = shape_constants()
    arrays = {
        "wstream": lay_out(a),
        "wba": np.ascontiguousarray(a["w_in"][0][:, 5632:5664].reshape(8, 128, 32).transpose(1, 0, 2).reshape(128, 256)),
        "consts": cst,
        "vecs": vectors(a, inv2),
        "cossin": cossin,
        "pos": np.ascontiguousarray(np.broadcast_to(a["positions_2"], (128, S))),
        "xT": feature_major(a["x"][0]),
        "pT": feature_major(a["p"][0, 0]),
    }
    nc = _bacc.Bacc("TRN2", target_bir_lowering=False, num_devices=1)
    args = [nc.dram_tensor(n, v.shape, mybir.dt.from_np(v.dtype), kind="ExternalInput").ap() for n, v in arrays.items()]
    out = nc.dram_tensor("out_0", (128, KT, S), F32, kind="ExternalOutput").ap()
    build(nc, *args, out)
    r = _run(nc, [arrays], core_ids=[0])
    got = r.results[0]["out_0"]
    return np.ascontiguousarray(got.transpose(1, 0, 2).reshape(1024, S).T)[None]
```
